# Optimizing a Trainium2 kernel written in Bass

```python
import jax, jax.numpy as jnp
from jax import lax
import numpy as np

D_MODEL = 1024
BATCH = 1
SEQ = 256
DEPTH = 2
DEC_BATCH = 8
DEC_SEQ = 4
PAST_LEN = 2048
PAGE_SIZE = 128

N_A_LAYERS = DEPTH // 2
N_B_LAYERS = DEPTH - N_A_LAYERS
N_DENSE = (DEPTH + 1) // 2
N_MOE = DEPTH // 2
RW_HEAD_DIM = 64
RW_HEADS = D_MODEL // RW_HEAD_DIM
RW_LORA_DECAY = 64
RW_LORA_ICLR = 64
RW_LORA_GATE = 160
RW_GN_EPS = 64e-5
N_HEADS = 16
HEAD_DIM = D_MODEL // N_HEADS
N_KV_HEADS = 4
HEADS_PER_KV = N_HEADS // N_KV_HEADS
N_BRANCH = 3
CMP_BLOCK = 32
CMP_STRIDE = 16
CMP_RATIO = CMP_BLOCK // CMP_STRIDE
CMP_HIDDEN = HEAD_DIM
SLC_BLOCK = 64
SLC_TOP = 16
WINDOW = 512
SLC_QBLOCK = 64
WIN_QBLOCK = 128
ATTN_SCALE = HEAD_DIM ** -0.5
D_FF = 2816
N_EXPERTS = 8
TOP_K = 2
MOE_BLOCK = 128
RMS_EPS = 1e-6

kernel_name = 'rwkv7_yoco_nsa_moe_decode_step'

def rmsnorm(x, g):
    xf = x.astype(jnp.float32)
    y = xf * lax.rsqrt(jnp.mean(xf * xf, -1, keepdims=True) + RMS_EPS)
    return (y * g.astype(jnp.float32)).astype(x.dtype)

def masked_softmax(s, mask):
    s = jnp.where(mask, s.astype(jnp.float32), -jnp.inf)
    m = jnp.max(s, -1, keepdims=True)
    m = jnp.where(jnp.isfinite(m), m, 0.0)
    e = jnp.exp(s - m)
    return e / jnp.maximum(jnp.sum(e, -1, keepdims=True), 1e-30)

def swiglu(x, wg, wu, wd):
    return (jax.nn.silu(x @ wg) * (x @ wu)) @ wd

def moe_swiglu(x, w_router, wg, wu, wd):
    shp = x.shape
    xt = x.reshape(-1, D_MODEL)
    n = xt.shape[0]
    logits = (xt @ w_router).astype(jnp.float32)
    top_v, top_e = lax.top_k(logits, TOP_K)
    gates = jax.nn.softmax(top_v, -1)
    p = n * TOP_K
    flat_e = top_e.reshape(p)
    flat_tok = jnp.repeat(jnp.arange(n, dtype=jnp.int32), TOP_K)
    flat_g = gates.reshape(p)
    order = jnp.argsort(flat_e)
    se = flat_e[order]
    counts = jnp.zeros((N_EXPERTS,), jnp.int32).at[flat_e].add(1)
    padded = (counts + MOE_BLOCK - 1) // MOE_BLOCK * MOE_BLOCK
    pad_end = jnp.cumsum(padded)
    pad_start = pad_end - padded
    start = jnp.cumsum(counts) - counts
    dest = pad_start[se] + jnp.arange(p, dtype=jnp.int32) - start[se]
    n_blocks = -(-p // MOE_BLOCK) + N_EXPERTS
    cap = n_blocks * MOE_BLOCK
    buf_tok = jnp.full((cap,), n, jnp.int32).at[dest].set(flat_tok[order])
    buf_gate = jnp.zeros((cap,), jnp.float32).at[dest].set(flat_g[order])
    block_e = jnp.minimum(jnp.searchsorted(pad_end, jnp.arange(n_blocks) * MOE_BLOCK, side='right'), N_EXPERTS - 1)
    x_pad = jnp.concatenate([xt, jnp.zeros((1, D_MODEL), xt.dtype)], 0)

    def expert_block(args):
        tok, e = args
        xb = x_pad[tok]
        return (jax.nn.silu(xb @ wg[e]) * (xb @ wu[e])) @ wd[e]

    yb = lax.map(expert_block, (buf_tok.reshape(n_blocks, MOE_BLOCK), block_e))
    y = jnp.zeros((n + 1, D_MODEL), jnp.float32).at[buf_tok].add(yb.reshape(cap, D_MODEL).astype(jnp.float32) * buf_gate[:, None])
    return y[:n].astype(x.dtype).reshape(shp)

def rwkv7_time_mix(x, shift0, wkv0, mix, vec, w_rkv, w_o, dw1, dw2, aw1, aw2, gw1, gw2):
    B, T, D = x.shape
    f32 = jnp.float32
    xx = jnp.concatenate([shift0[:, None, :].astype(x.dtype), x[:, :-1]], axis=1) - x
    xr, xw, xk, xv, xa, xg = (x + xx * mix[i] for i in range(6))
    w0, a0, k_k, k_a, r_k, ln_w, ln_b = (vec[i] for i in range(7))
    heads = lambda t: t.reshape(B, T, RW_HEADS, RW_HEAD_DIM).astype(f32)
    r = heads(xr @ w_rkv[0])
    k = xk @ w_rkv[1]
    v = heads(xv @ w_rkv[2])
    log_w = -jax.nn.softplus(-(w0 + jnp.tanh(xw @ dw1) @ dw2)) - 0.5
    decay = jnp.exp(-jnp.exp(heads(log_w)))
    a = jax.nn.sigmoid(a0 + (xa @ aw1) @ aw2)
    g = jax.nn.sigmoid(xg @ gw1) @ gw2
    kk = heads(k * k_k)
    kk = kk * lax.rsqrt(jnp.maximum(jnp.sum(kk * kk, -1, keepdims=True), 1e-24))
    k = heads(k * (1 + (a - 1) * k_a))
    a = heads(a)

    def step(S, inp):
        r_t, w_t, k_t, v_t, kk_t, a_t = inp
        sa = jnp.einsum('bhvk,bhk->bhv', S, -kk_t)
        S = S * w_t[:, :, None, :] + sa[..., None] * (kk_t * a_t)[:, :, None, :] + v_t[..., None] * k_t[:, :, None, :]
        return S, jnp.einsum('bhvk,bhk->bhv', S, r_t)

    seq = tuple(jnp.swapaxes(t, 0, 1) for t in (r, decay, k, v, kk, a))
    S_T, y = lax.scan(step, wkv0.astype(f32), seq)
    y = jnp.swapaxes(y, 0, 1)
    mu = jnp.mean(y, -1, keepdims=True)
    var = jnp.mean(jnp.square(y - mu), -1, keepdims=True)
    y = ((y - mu) * lax.rsqrt(var + RW_GN_EPS)).reshape(B, T, D) * ln_w.astype(f32) + ln_b.astype(f32)
    bonus = jnp.sum(r * k * r_k.reshape(RW_HEADS, RW_HEAD_DIM).astype(f32), -1, keepdims=True) * v
    y = y + bonus.reshape(B, T, D)
    out = (y * g.astype(f32)).astype(x.dtype) @ w_o
    return out, x[:, -1], S_T.astype(wkv0.dtype)

def shared_kv_rows(h, kv_norm_g, w_kv, k_norm_g):
    B, T, _ = h.shape
    kv = (rmsnorm(h, kv_norm_g) @ w_kv).reshape(B, T, N_BRANCH, 2, N_KV_HEADS, HEAD_DIM)
    normed = lambda c: jnp.stack([rmsnorm(kv[:, :, c, 0], k_norm_g[c]), kv[:, :, c, 1]], axis=2)
    return kv[:, :, 0], normed(1), normed(2)

def compress(rows, pe, w1, w2):
    lead = rows.shape[:-3]
    n_sub = rows.shape[-3] // CMP_STRIDE
    n_cmp = n_sub - CMP_RATIO + 1
    sub = rows[..., :n_sub * CMP_STRIDE, :, :].reshape(lead + (n_sub, CMP_STRIDE, N_KV_HEADS, HEAD_DIM))
    pe_r = pe.reshape(CMP_RATIO, CMP_STRIDE, HEAD_DIM)
    w1_r = w1.reshape(CMP_RATIO, CMP_STRIDE, HEAD_DIM, CMP_HIDDEN)
    pre = sum(jnp.einsum('...nsgd,sdh->...ngh', sub[..., j:j + n_cmp, :, :, :] + pe_r[j][:, None, :], w1_r[j])
              for j in range(CMP_RATIO))
    return jax.nn.silu(pre) @ w2

def compressed_kv(rows, k_norm_g0, cmp_pe, cmp_w1, cmp_w2):
    kc = rmsnorm(compress(rows[..., 0, :, :], cmp_pe[0], cmp_w1[0], cmp_w2[0]), k_norm_g0)
    vc = compress(rows[..., 1, :, :], cmp_pe[1], cmp_w1[1], cmp_w2[1])
    return kc, vc

def cmp_to_slc(n_cmp, n_slc):
    c0 = jnp.arange(n_cmp)[:, None] * CMP_STRIDE
    s0 = jnp.arange(n_slc)[None, :] * SLC_BLOCK
    return ((c0 < s0 + SLC_BLOCK) & (c0 + CMP_BLOCK > s0)).astype(jnp.float32)

def nsa_cmp_slc(q, q_pos, kc, vc, gather_slc, n_slc):
    Q = q.shape[0]
    n_cmp = kc.shape[0]
    qg = q.reshape(Q, N_KV_HEADS, HEADS_PER_KV, HEAD_DIM)
    s = jnp.einsum('qgid,ngd->qgin', qg, kc) * ATTN_SCALE
    c_end = jnp.arange(n_cmp) * CMP_STRIDE + CMP_BLOCK - 1
    p = masked_softmax(s, (c_end[None, :] <= q_pos[:, None])[:, None, None, :])
    o_cmp = jnp.einsum('qgin,ngd->qgid', p.astype(vc.dtype), vc)
    imp = jnp.einsum('qgin,nj->qgj', p, cmp_to_slc(n_cmp, n_slc))
    blk = jnp.arange(n_slc)[None, None, :]
    cur = (q_pos // SLC_BLOCK)[:, None, None]
    forced = (blk == 0) | (blk == cur) | (blk == cur - 1)
    score = jnp.where(blk <= cur, jnp.where(forced, jnp.inf, imp), -jnp.inf)
    _, idx = lax.top_k(score, min(SLC_TOP, n_slc))
    n_sel = idx.shape[-1]
    kpos = idx[..., None] * SLC_BLOCK + jnp.arange(SLC_BLOCK)
    kv = gather_slc(kpos)
    mask = (kpos <= q_pos[:, None, None, None]).reshape(Q, N_KV_HEADS, 1, n_sel * SLC_BLOCK)
    s2 = jnp.einsum('qgid,qgnkd->qgink', qg, kv[..., 0, :]) * ATTN_SCALE
    p2 = masked_softmax(s2.reshape(Q, N_KV_HEADS, HEADS_PER_KV, n_sel * SLC_BLOCK), mask)
    v_sel = kv[..., 1, :].reshape(Q, N_KV_HEADS, n_sel * SLC_BLOCK, HEAD_DIM)
    o_slc = jnp.einsum('qgim,qgmd->qgid', p2.astype(v_sel.dtype), v_sel)
    return o_cmp.reshape(Q, N_HEADS, HEAD_DIM), o_slc.reshape(Q, N_HEADS, HEAD_DIM)

def band_mask(q_pos, k_pos):
    d = q_pos[:, None] - k_pos[None, :]
    return (d >= 0) & (d < WINDOW) & (k_pos[None, :] >= 0)

def gqa_attend(q, k, v, mask):
    B, Q = q.shape[:2]
    qg = q.reshape(B, Q, N_KV_HEADS, HEADS_PER_KV, HEAD_DIM)
    s = jnp.einsum('bqgid,bkgd->bqgik', qg, k) * ATTN_SCALE
    p = masked_softmax(s, mask[None, :, None, None, :])
    o = jnp.einsum('bqgik,bkgd->bqgid', p.astype(v.dtype), v)
    return o.reshape(B, Q, N_HEADS, HEAD_DIM)

def window_prompt(q, kv):
    B, T = q.shape[:2]
    kvp = jnp.concatenate([jnp.zeros((B, WINDOW) + kv.shape[2:], kv.dtype), kv], axis=1)

    def blk(i):
        q0 = i * WIN_QBLOCK
        qi = lax.dynamic_slice_in_dim(q, q0, WIN_QBLOCK, axis=1)
        kvi = lax.dynamic_slice_in_dim(kvp, q0, WIN_QBLOCK + WINDOW, axis=1)
        q_pos = q0 + jnp.arange(WIN_QBLOCK)
        k_pos = q0 - WINDOW + jnp.arange(WIN_QBLOCK + WINDOW)
        return gqa_attend(qi, kvi[:, :, 0], kvi[:, :, 1], band_mask(q_pos, k_pos))

    o = lax.map(blk, jnp.arange(T // WIN_QBLOCK))
    return jnp.moveaxis(o, 0, 1).reshape(B, T, N_HEADS, HEAD_DIM)

def query_side(hn, w_qg, q_norm_g):
    B, T, _ = hn.shape
    proj = hn @ w_qg
    q = rmsnorm(proj[..., :N_HEADS * HEAD_DIM].reshape(B, T, N_HEADS, HEAD_DIM), q_norm_g)
    gates = jax.nn.sigmoid(proj[..., N_HEADS * HEAD_DIM:].astype(jnp.float32)).reshape(B, T, N_BRANCH, N_HEADS)
    return q, gates

def merge_branches(gates, o_cmp, o_slc, o_win, w_o):
    f32 = jnp.float32
    o = (gates[..., 0, :, None] * o_cmp.astype(f32) + gates[..., 1, :, None] * o_slc.astype(f32)
         + gates[..., 2, :, None] * o_win.astype(f32)).astype(w_o.dtype)
    B, T = o.shape[:2]
    return o.reshape(B, T, N_HEADS * HEAD_DIM) @ w_o

def nsa_prompt(hn, kc, vc, slc_kv, win_kv, w_qg, q_norm_g, w_o):
    B, T, _ = hn.shape
    q, gates = query_side(hn, w_qg, q_norm_g)
    n_slc = T // SLC_BLOCK
    n_qb = T // SLC_QBLOCK
    g_ar = jnp.arange(N_KV_HEADS)[None, :, None, None]

    def item(args):
        b, qb = args
        q0 = qb * SLC_QBLOCK
        q_blk = lax.dynamic_slice_in_dim(q[b], q0, SLC_QBLOCK, axis=0)
        q_pos = q0 + jnp.arange(SLC_QBLOCK)
        gather = lambda kpos: slc_kv[b, kpos, :, g_ar, :]
        return nsa_cmp_slc(q_blk, q_pos, kc[b], vc[b], gather, n_slc)

    b_ids = jnp.repeat(jnp.arange(B), n_qb)
    qb_ids = jnp.tile(jnp.arange(n_qb), B)
    o_cmp, o_slc = lax.map(item, (b_ids, qb_ids))
    o_cmp = o_cmp.reshape(B, T, N_HEADS, HEAD_DIM)
    o_slc = o_slc.reshape(B, T, N_HEADS, HEAD_DIM)
    o_win = window_prompt(q, win_kv)
    return merge_branches(gates, o_cmp, o_slc, o_win, w_o)

def sample_compressed_kv(cache_cmp_kv, page_table, cmp_new, k_norm_g0, cmp_pe, cmp_w1, cmp_w2):
    def per_seq(args):
        pt_row, new_rows = args
        past = cache_cmp_kv[pt_row]
        past = past.reshape((-1,) + past.shape[2:])
        return compressed_kv(jnp.concatenate([past, new_rows.astype(past.dtype)], 0), k_norm_g0, cmp_pe, cmp_w1, cmp_w2)
    return lax.map(per_seq, (page_table, cmp_new))

def nsa_sample(hn, kc, vc, slc_new, win_all, wb, cache_slc_kv, page_table, w_qg, q_norm_g, w_o):
    B, S, _ = hn.shape
    q, gates = query_side(hn, w_qg, q_norm_g)
    q_pos = PAST_LEN + jnp.arange(S)
    n_slc = (PAST_LEN + S - 1) // SLC_BLOCK + 1
    g_ar = jnp.arange(N_KV_HEADS)[None, :, None, None]

    def per_seq(args):
        q_b, kc_b, vc_b, pt_b, new_b = args

        def gather(kpos):
            kp = jnp.minimum(kpos, PAST_LEN - 1)
            from_pool = cache_slc_kv[pt_b[kp // PAGE_SIZE], kp % PAGE_SIZE, :, g_ar, :]
            from_new = new_b[jnp.clip(kpos - PAST_LEN, 0, S - 1), :, g_ar, :].astype(from_pool.dtype)
            return jnp.where((kpos < PAST_LEN)[..., None, None], from_pool, from_new)

        return nsa_cmp_slc(q_b, q_pos, kc_b, vc_b, gather, n_slc)

    o_cmp, o_slc = lax.map(per_seq, (q, kc, vc, page_table, slc_new))
    k_pos = PAST_LEN - wb + jnp.arange(wb + S)
    o_win = gqa_attend(q, win_all[:, :, 0], win_all[:, :, 1], band_mask(q_pos, k_pos))
    return merge_branches(gates, o_cmp, o_slc, o_win, w_o)

def setup_inputs(seed: int = 0) -> dict:
    key = jax.random.key(seed)
    ks = iter(jax.random.split(key, 64))
    f32 = jnp.float32
    nrm = lambda shape, scale: jax.random.normal(next(ks), shape, f32) * scale
    n_pages = PAST_LEN // PAGE_SIZE
    n_used = DEC_BATCH * n_pages
    n_pool = n_used + max(1, n_used // 4)
    page_table = jax.random.permutation(next(ks), n_pool)[:n_used].reshape(DEC_BATCH, n_pages).astype(jnp.int32)
    inv = D_MODEL ** -0.5
    kv_width = N_BRANCH * 2 * N_KV_HEADS * HEAD_DIM
    base = jnp.array([0.0, 0.0, 0.85, 1.0, 0.0, 1.0, 0.0], f32)[None, :, None]
    spread = jnp.array([0.0, 0.3, 0.05, 0.05, 0.1, 0.02, 0.02], f32)[None, :, None]
    rw_vec = base + spread * nrm((N_A_LAYERS, 7, D_MODEL), 1.0)
    rw_vec = rw_vec.at[:, 0].set(jax.random.uniform(next(ks), (N_A_LAYERS, D_MODEL), f32, -3.0, 1.0))
    return {
        'x_prompt': nrm((BATCH, SEQ, D_MODEL), 1.0),
        'x_sample': nrm((DEC_BATCH, DEC_SEQ, D_MODEL), 1.0),
        'cache_cmp_kv': nrm((n_pool, PAGE_SIZE, 2, N_KV_HEADS, HEAD_DIM), 1.0),
        'cache_slc_kv': nrm((n_pool, PAGE_SIZE, 2, N_KV_HEADS, HEAD_DIM), 1.0),
        'state_win_kv': nrm((DEC_BATCH, min(WINDOW, PAST_LEN), 2, N_KV_HEADS, HEAD_DIM), 1.0),
        'state_wkv': nrm((N_A_LAYERS, DEC_BATCH, RW_HEADS, RW_HEAD_DIM, RW_HEAD_DIM), 0.5),
        'state_shift': nrm((N_A_LAYERS, DEC_BATCH, D_MODEL), 1.0),
        'page_table': page_table,
        'norm_g': 1.0 + nrm((DEPTH, 2, D_MODEL), 0.02),
        'rw_mix': jax.random.uniform(next(ks), (N_A_LAYERS, 6, D_MODEL), f32),
        'rw_vec': rw_vec,
        'rw_w_rkv': nrm((N_A_LAYERS, 3, D_MODEL, D_MODEL), inv),
        'rw_w_o': nrm((N_A_LAYERS, D_MODEL, D_MODEL), inv),
        'rw_decay_w1': nrm((N_A_LAYERS, D_MODEL, RW_LORA_DECAY), inv),
        'rw_decay_w2': nrm((N_A_LAYERS, RW_LORA_DECAY, D_MODEL), 0.1 * RW_LORA_DECAY ** -0.5),
        'rw_iclr_w1': nrm((N_A_LAYERS, D_MODEL, RW_LORA_ICLR), inv),
        'rw_iclr_w2': nrm((N_A_LAYERS, RW_LORA_ICLR, D_MODEL), 0.1 * RW_LORA_ICLR ** -0.5),
        'rw_gate_w1': nrm((N_A_LAYERS, D_MODEL, RW_LORA_GATE), inv),
        'rw_gate_w2': nrm((N_A_LAYERS, RW_LORA_GATE, D_MODEL), RW_LORA_GATE ** -0.5),
        'ffn_w_gate': nrm((N_DENSE, D_MODEL, D_FF), inv),
        'ffn_w_up': nrm((N_DENSE, D_MODEL, D_FF), inv),
        'ffn_w_down': nrm((N_DENSE, D_FF, D_MODEL), D_FF ** -0.5),
        'moe_router': nrm((N_MOE, D_MODEL, N_EXPERTS), inv),
        'moe_w_gate': nrm((N_MOE, N_EXPERTS, D_MODEL, D_FF), inv),
        'moe_w_up': nrm((N_MOE, N_EXPERTS, D_MODEL, D_FF), inv),
        'moe_w_down': nrm((N_MOE, N_EXPERTS, D_FF, D_MODEL), D_FF ** -0.5),
        'kv_norm_g': 1.0 + nrm((D_MODEL,), 0.02),
        'w_kv': nrm((D_MODEL, kv_width), inv),
        'k_norm_g': 1.0 + nrm((N_BRANCH, HEAD_DIM), 0.02),
        'cmp_pe': nrm((2, CMP_BLOCK, HEAD_DIM), 0.1),
        'cmp_w1': nrm((2, CMP_BLOCK, HEAD_DIM, CMP_HIDDEN), (CMP_BLOCK * HEAD_DIM) ** -0.5),
        'cmp_w2': nrm((2, CMP_HIDDEN, HEAD_DIM), CMP_HIDDEN ** -0.5),
        'w_qg': nrm((N_B_LAYERS, D_MODEL, N_HEADS * HEAD_DIM + N_BRANCH * N_HEADS), inv),
        'q_norm_g': 1.0 + nrm((N_B_LAYERS, HEAD_DIM), 0.02),
        'w_o': nrm((N_B_LAYERS, N_HEADS * HEAD_DIM, D_MODEL), (N_HEADS * HEAD_DIM) ** -0.5),
    }

def reference(x_prompt, x_sample, cache_cmp_kv, cache_slc_kv, state_win_kv, state_wkv, state_shift, page_table,
              norm_g, rw_mix, rw_vec, rw_w_rkv, rw_w_o, rw_decay_w1, rw_decay_w2, rw_iclr_w1, rw_iclr_w2,
              rw_gate_w1, rw_gate_w2, ffn_w_gate, ffn_w_up, ffn_w_down, moe_router, moe_w_gate, moe_w_up,
              moe_w_down, kv_norm_g, w_kv, k_norm_g, cmp_pe, cmp_w1, cmp_w2, w_qg, q_norm_g, w_o):
    hp, hs = x_prompt, x_sample
    B, T, _ = hp.shape
    wb = state_win_kv.shape[1]
    wkv_p, wkv_s, shift_p, shift_s = [], [], [], []
    for layer in range(DEPTH):
        if layer < N_A_LAYERS:
            rw = (rw_mix[layer], rw_vec[layer], rw_w_rkv[layer], rw_w_o[layer], rw_decay_w1[layer],
                  rw_decay_w2[layer], rw_iclr_w1[layer], rw_iclr_w2[layer], rw_gate_w1[layer], rw_gate_w2[layer])
            o, sh, st = rwkv7_time_mix(rmsnorm(hp, norm_g[layer, 0]), jnp.zeros((B, D_MODEL), hp.dtype),
                                       jnp.zeros((B, RW_HEADS, RW_HEAD_DIM, RW_HEAD_DIM), hp.dtype), *rw)
            hp = hp + o
            shift_p.append(sh)
            wkv_p.append(st)
            o, sh, st = rwkv7_time_mix(rmsnorm(hs, norm_g[layer, 0]), state_shift[layer], state_wkv[layer], *rw)
            hs = hs + o
            shift_s.append(sh)
            wkv_s.append(st)
        else:
            if layer == N_A_LAYERS:
                cmp_p, slc_p, win_p = shared_kv_rows(hp, kv_norm_g, w_kv, k_norm_g)
                kc_p, vc_p = compressed_kv(cmp_p, k_norm_g[0], cmp_pe, cmp_w1, cmp_w2)
                cmp_s, slc_s, win_s = shared_kv_rows(hs, kv_norm_g, w_kv, k_norm_g)
                kc_s, vc_s = sample_compressed_kv(cache_cmp_kv, page_table, cmp_s, k_norm_g[0], cmp_pe, cmp_w1, cmp_w2)
                win_all_s = jnp.concatenate([state_win_kv, win_s.astype(state_win_kv.dtype)], axis=1)
            j = layer - N_A_LAYERS
            hp = hp + nsa_prompt(rmsnorm(hp, norm_g[layer, 0]), kc_p, vc_p, slc_p, win_p, w_qg[j], q_norm_g[j], w_o[j])
            hs = hs + nsa_sample(rmsnorm(hs, norm_g[layer, 0]), kc_s, vc_s, slc_s, win_all_s, wb, cache_slc_kv,
                                 page_table, w_qg[j], q_norm_g[j], w_o[j])
        f = layer // 2
        if layer % 2 == 0:
            hp = hp + swiglu(rmsnorm(hp, norm_g[layer, 1]), ffn_w_gate[f], ffn_w_up[f], ffn_w_down[f])
            hs = hs + swiglu(rmsnorm(hs, norm_g[layer, 1]), ffn_w_gate[f], ffn_w_up[f], ffn_w_down[f])
        else:
            hp = hp + moe_swiglu(rmsnorm(hp, norm_g[layer, 1]), moe_router[f], moe_w_gate[f], moe_w_up[f], moe_w_down[f])
            hs = hs + moe_swiglu(rmsnorm(hs, norm_g[layer, 1]), moe_router[f], moe_w_gate[f], moe_w_up[f], moe_w_down[f])
    keep_p = min(WINDOW, T)
    return (hp, hs, cmp_p, cmp_s, slc_p, slc_s, win_p[:, T - keep_p:], win_all_s[:, win_all_s.shape[1] - wb:],
            jnp.stack(wkv_p), jnp.stack(wkv_s), jnp.stack(shift_p), jnp.stack(shift_s))


_drawn_inputs = setup_inputs


def setup_inputs(seed=0):
    import zlib

    import numpy as np

    out = dict(_drawn_inputs(seed))
    spreads = {}
    factors = {'rw_decay_w1': 3.521,
     'rw_decay_w2': 3.118,
     'kv_norm_g': 3.097,
     'k_norm_g': 3.82,
     'q_norm_g': 8.0}
    for name, (base, spread) in spreads.items():
        noise = np.random.default_rng([zlib.crc32(name.encode()), seed]).standard_normal(out[name].shape)
        drawn = base * np.exp(spread * noise) if base else spread * noise
        out[name] = __import__('jax').numpy.asarray(drawn.astype(out[name].dtype))
    for name, factor in factors.items():
        out[name] = (out[name] * factor).astype(out[name].dtype)
    return out
```

```python
import math
from contextlib import ExitStack

import concourse.bass as bass
from concourse import mybir

ALU = mybir.AluOpType
ACT = mybir.ActivationFunctionType
F32 = mybir.dt.float32
I32 = mybir.dt.int32
AX = mybir.AxisListType.X

P = 128
D = 1024
DC = D // P
NP = 256
NB, DS = 8, 4
NS = NB * DS
NT = NP + NS
HD = 64
NH = D // HD
CH = 64
F_FF = 2816
FC = F_FF // P
NE = 8
RMS_EPS = 1e-6
GN_EPS = 64e-5
KAPPA = math.exp(-0.5)
NEG = -1e30
SCALE = HD ** -0.5

C_MIX = 0
C_VEC = 48
C_NG = 128
C_KVG = 160
C_SH = 168
C_KN = 256
NCOL = 260
V_W0, V_A0, V_KK, V_KA, V_RK, V_LNW, V_LNB = (C_VEC + 8 * i for i in range(7))


class Chain:

    def __init__(self, eng, sem, value=0):
        self.eng, self.sem, self.value = eng, sem, value

    def __call__(self, ins):
        self.value += 1
        ins.then_inc(self.sem, 1)
        self.eng.wait_ge(self.sem, self.value)


class Scope:

    def __init__(self, nc, name):
        self.nc, self.name, self.ctx = nc, name, ExitStack()

    def __enter__(self):
        self.ctx.__enter__()
        return self

    def __exit__(self, *a):
        return self.ctx.__exit__(*a)

    def sb(self, name, shape, dt=F32, side="left"):
        return self.ctx.enter_context(self.nc.sbuf_tensor(f"{self.name}.{name}", shape, dt, side=side))

    def bank(self, name, shape=(P, 512)):
        return self.ctx.enter_context(self.nc.psum_tensor(f"{self.name}.{name}", list(shape), F32))

    def sem(self, name):
        sem = self.ctx.enter_context(self.nc.semaphore(f"{self.name}.{name}"))
        self.ctx.callback(self.nc.gpsimd.sem_clear, sem)
        return sem

    def block(self):
        return self.ctx.enter_context(self.nc.Block())


def stage_load(nc, G, io):
    with Scope(nc, "load") as s:
        xr = s.sb("x_rows", [P, 3, D])
        va = s.sb("vec_a", [P, P])
        vb = s.sb("vec_b", [P, P])
        vc = s.sb("vec_c", [4, P])
        x_in, vec_in = s.sem("x_in"), s.sem("vec_in")
        const0, const1 = s.sem("const_filled"), s.sem("const_ready")
        turned, copied = s.sem("turned"), s.sem("copied")
        bank = [s.bank(f"b{i}") for i in range(6)]
        with nc.Block() as block:
            @block.sync
            def _(sp):
                sp.dma_start(xr[:, 0:2, :], io["x_prompt"][0].rearrange("(n p) d -> p n d", p=P)).then_inc(x_in, 16)
                sp.dma_start(xr[0:NS, 2, :], io["x_sample"].rearrange("b t d -> (b t) d")).then_inc(x_in, 16)

            @block.scalar
            def _(act):
                rows = lambda name: io[name].rearrange("a i (c p) -> (a i c) p", p=P)
                for out, src in ((va[0:48, :], rows("rw_mix")), (va[48:104, :], rows("rw_vec")),
                                 (vb[0:32, :], rows("norm_g")),
                                 (vb[32:40, :], io["kv_norm_g"].rearrange("(c p) -> c p", p=P)),
                                 (vb[40:104, :], rows("state_shift"))):
                    act.dma_start(out, src).then_inc(vec_in, 16)
                for g2 in range(2):
                    act.dma_start(vc[0:3, HD * g2:HD * g2 + HD], io["k_norm_g"]).then_inc(vec_in, 16)
                    act.dma_start(vc[3:4, HD * g2:HD * g2 + HD], io["q_norm_g"]).then_inc(vec_in, 16)
                for n in range(2, 4):
                    act.wait_ge(turned, n + 1)
                    nc.scalar.copy(G.h[:, 4 * (n % 2):4 * (n % 2) + 4, P:2 * P],
                                   bank[n][:, :].rearrange("p (c t) -> p c t", t=P)).then_inc(copied, 1)

            @block.gpsimd
            def _(pool):
                c = Chain(pool, const0)
                c(nc.gpsimd.memset(G.ident[:, :], 0.0))
                c(nc.gpsimd.memset(G.ones[:, :], 1.0))
                c(nc.gpsimd.memset(G.eps[:, :], RMS_EPS))
                c(nc.gpsimd.memset(G.blk[:, :], 0.0))
                for q in range(2):
                    c(nc.gpsimd.memset(G.blk[HD * q:HD * q + HD, HD * q:HD * q + HD], 1.0))
                c(nc.gpsimd.affine_select(out=G.ident[:, :], in_=G.ident[:, :], compare_op=ALU.not_equal, fill=1.0,
                                          base=0, pattern=[[-1, P]], channel_multiplier=1))
                nc.gpsimd.memset(G.gneps[:, :], GN_EPS).then_inc(const1, 1)

            @block.tensor
            def _(pe):
                pe.wait_ge(const1, 1)
                pe.wait_ge(x_in, 32)
                for n in range(4):
                    for c in range(4):
                        last = nc.tensor.transpose(bank[n][:, P * c:P * c + P],
                                                   xr[:, n // 2, P * (4 * (n % 2) + c):P * (4 * (n % 2) + c) + P],
                                                   G.ident[:, :])
                    last.then_inc(turned, 1)
                for c in range(DC):
                    last = nc.tensor.transpose(bank[4][:, NS * c:NS * c + NS], xr[0:NS, 2, P * c:P * c + P],
                                               G.ident[0:NS, 0:NS])
                last.then_inc(turned, 1)
                pe.wait_ge(vec_in, 9 * 16)
                nc.tensor.transpose(bank[5][:, 0:104], va[0:104, :], G.ident[0:104, 0:104])
                nc.tensor.transpose(bank[5][:, 128:232], vb[0:104, :], G.ident[0:104, 0:104])
                nc.tensor.transpose(bank[5][:, 256:260], vc[:, :], G.ident[0:4, 0:4]).then_inc(turned, 1)

            @block.vector
            def _(dve):
                for n in range(2):
                    dve.wait_ge(turned, n + 1)
                    nc.vector.tensor_copy(G.h[:, 4 * n:4 * n + 4, 0:P], bank[n][:, :].rearrange("p (c t) -> p c t", t=P))
                dve.wait_ge(turned, 5)
                nc.vector.tensor_copy(G.h[:, :, NP:NT], bank[4][:, 0:NS * DC].rearrange("p (c t) -> p c t", t=NS))
                dve.wait_ge(turned, 6)
                for a, b in ((0, 104), (128, 232), (256, 260)):
                    nc.vector.tensor_copy(G.pv[:, a:b], bank[5][:, a:b])


def stage_norm(nc, G, name, gamma, xn, ahead, work, bank):
    with Scope(nc, name) as s:
        sq, std, rstd = xn, work[:, 0], work[:, 1]
        squared, summed, rooted, inv = (s.sem(x) for x in ("squared", "summed", "rooted", "inverted"))
        ss = bank[:, 0:NT]
        block = s.block()

        @block.sync
        def _(sp):
            ahead(sp)

        @block.scalar
        def _(act):
            for c in range(DC):
                nc.scalar.activation(sq[:, c, :], G.h[:, c, :], ACT.Square).then_inc(squared, 1)
            act.wait_ge(summed, 1)
            nc.scalar.activation(std, ss, ACT.Sqrt, scale=1.0 / D, bias=G.eps[:, 0:1]).then_inc(rooted, 1)

        @block.tensor
        def _(pe):
            for c in range(DC):
                pe.wait_ge(squared, c + 1)
                last = nc.tensor.matmul(ss, G.ones[:, :], sq[:, c, :], start=(c == 0), stop=(c == DC - 1))
            last.then_inc(summed, 1)

        @block.vector
        def _(dve):
            dve.wait_ge(rooted, 1)
            nc.vector.reciprocal(rstd, std).then_inc(inv, 1)
            dve.wait_ge(inv, 1)
            for c in range(DC):
                nc.vector.scalar_tensor_tensor(out=xn[:, c, :], in0=G.h[:, c, :], scalar=G.pv[:, gamma + c:gamma + c + 1],
                                               in1=rstd, op0=ALU.mult, op1=ALU.mult)


def stage_rwkv_in(nc, G, R, io, idle):
    with Scope(nc, "rin") as s:
        xn = s.sb("xn", [P, DC, NT])
        xx = s.sb("xx", [P, DC, NT])
        xm = s.sb("xm", [P, 2, DC, NT])
        big = s.sb("w_rkv", [P, 2, DC, D])
        w1 = {"w": s.sb("dw1", [P, DC, 64]), "a": s.sb("aw1", [P, DC, 64]), "g": s.sb("gw1", [P, DC, 160])}
        w2 = {"w": s.sb("dw2", [64, D]), "a": s.sb("aw2", [64, D]), "g": s.sb("gw2", [P, D])}
        g2b = R.v[0:32].rearrange("p c t -> p (c t)")[:, 0:D]
        mid = R.r[:, 0:4, :]
        lastrow = s.sb("shift_cols", [P, DC, 9])
        shrows = idle[0:9].rearrange("p c t -> p (c t)")[:, 0:D]
        bank = [s.bank(f"b{i}") for i in range(8)]
        small_in, rkv_in = s.sem("small_in"), [s.sem(f"rkv_in{i}") for i in range(2)]

        def load_rkv(sp, i):
            sp.dma_start(big[:, i % 2], io["rw_w_rkv"][0, i].rearrange("(c p) n -> p c n", p=P)).then_inc(rkv_in[i % 2], 16)

        def ahead(sp):
            for n, name in (("w", "rw_decay_w1"), ("a", "rw_iclr_w1"), ("g", "rw_gate_w1")):
                sp.dma_start(w1[n][:, :, :], io[name][0].rearrange("(c p) n -> p c n", p=P)).then_inc(small_in, 16)
            sp.dma_start(w2["w"][:, :], io["rw_decay_w2"][0]).then_inc(small_in, 16)
            sp.dma_start(w2["a"][:, :], io["rw_iclr_w2"][0]).then_inc(small_in, 16)
            sp.dma_start(w2["g"][:, :], io["rw_gate_w2"][0, 0:P, :]).then_inc(small_in, 16)
            sp.dma_start(g2b, io["rw_gate_w2"][0, P:160, :]).then_inc(small_in, 16)
            for i in range(2):
                load_rkv(sp, i)

        stage_norm(nc, G, "norm0", C_NG, xn, ahead, xm[:, 0, 0:2], bank[0])
        diff, mixed = s.sem("diff"), s.sem("mixed")
        done, evac = s.sem("group_done"), s.sem("group_copied")
        cols, shdma, const = s.sem("shift_cols"), s.sem("shift_out"), s.sem("const_step")
        ORDER = ("w", "a", "g", "r", "k", "v")
        READ = {"w": 3, "a": 12, "g": 22, "r": 38, "k": 46, "v": 54}
        MIX = {"r": 0, "w": 1, "k": 2, "v": 3, "a": 4, "g": 5}
        with nc.Block() as block:
            @block.gpsimd
            def _(pool):
                c = Chain(pool, const)
                c(nc.gpsimd.affine_select(out=G.mask_su[:, :], in_=G.blk[:, :], compare_op=ALU.is_gt, fill=0.0,
                                          base=0, pattern=[[1, P]], channel_multiplier=-1))
                c(nc.gpsimd.affine_select(out=G.mask_iu[:, :], in_=G.blk[:, :], compare_op=ALU.is_ge, fill=0.0,
                                          base=0, pattern=[[1, P]], channel_multiplier=-1))
                c(nc.gpsimd.memset(G.head_of[:, :, :], 0.0))
                c(nc.gpsimd.memset(G.to_head[:, :, :], 0.0))
                for q in range(2):
                    part = G.head_of[HD * q:HD * q + HD]
                    c(nc.gpsimd.affine_select(out=part, in_=part, compare_op=ALU.not_equal, fill=1.0, base=-q,
                                              pattern=[[-2, DC], [1, NH]], channel_multiplier=0))
                    part = G.to_head[:, :, HD * q:HD * q + HD]
                    c(nc.gpsimd.affine_select(out=part, in_=part, compare_op=ALU.not_equal, fill=1.0, base=-q,
                                              pattern=[[-2, DC], [0, HD]], channel_multiplier=1))
                for l in range(7):
                    m = 1 << l
                    view = G.level[:, l, :].rearrange("p (n m) -> p n m", m=m)
                    c(nc.gpsimd.affine_select(out=view, in_=G.ones[:, :].rearrange("p (n m) -> p n m", m=m),
                                              compare_op=ALU.is_ge, fill=0.0, base=0, pattern=[[-m, P // m], [0, m]],
                                              channel_multiplier=1))
                    c(nc.gpsimd.affine_select(out=view, in_=view, compare_op=ALU.is_ge, fill=0.0, base=m - 1,
                                              pattern=[[m, P // m], [0, m]], channel_multiplier=-1))
                for l in range(6):
                    c(nc.gpsimd.tensor_tensor(G.level[:, l, :], G.level[:, l + 1, :], G.level[:, l, :], ALU.subtract))
                    if l == 0:
                        c(nc.gpsimd.tensor_copy(G.level[:, 7, :], G.level[:, 0, :]))
                    c(nc.gpsimd.tensor_tensor(G.level[:, l, :], G.level[:, l, :], G.mask_su[:, :], ALU.mult))
                c(nc.gpsimd.tensor_tensor(G.level[:, 7, :], G.level[:, 7, :], G.level[:, 0, :], ALU.subtract))

            @block.sync
            def _(sp):
                sp.wait_ge(done, READ["r"])
                load_rkv(sp, 2)
                sp.wait_ge(evac, 2)
                sp.dma_start(io["shift_prompt"][0], shrows[0:1, :]).then_inc(shdma, 16)
                sp.dma_start(io["shift_sample"][0], shrows[1:9, :]).then_inc(shdma, 16)
                sp.wait_ge(shdma, 32)

            @block.vector
            def _(dve):
                xs = xn[:, :, NP:NT].rearrange("p c (b t) -> p c b t", t=DS)
                ds = xx[:, :, NP:NT].rearrange("p c (b t) -> p c b t", t=DS)
                nc.vector.tensor_copy(lastrow[:, :, 0:1], xn[:, :, NP - 1:NP])
                nc.vector.tensor_copy(lastrow[:, :, 1:9], xs[:, :, :, DS - 1]).then_inc(cols, 1)
                nc.vector.tensor_tensor(xx[:, :, 1:NP], xn[:, :, 0:NP - 1], xn[:, :, 1:NP], ALU.subtract)
                nc.vector.tensor_scalar(xx[:, :, 0:1], xn[:, :, 0:1], -1.0, None, ALU.mult)
                for c in range(DC):
                    nc.vector.tensor_tensor(ds[:, c, :, 1:DS], xs[:, c, :, 0:DS - 1], xs[:, c, :, 1:DS], ALU.subtract)
                sh0 = G.pv[:, C_SH:C_SH + 64].rearrange("p (b c) -> p c b", c=DC)
                nc.vector.tensor_tensor(ds[:, :, :, 0], sh0, xs[:, :, :, 0], ALU.subtract).then_inc(diff, 1)
                dve.wait_ge(diff, 1)
                for n, name in enumerate(ORDER):
                    if n >= 2:
                        dve.wait_ge(done, READ[ORDER[n - 2]])
                    for c in range(DC):
                        col = C_MIX + 8 * MIX[name] + c
                        last = nc.vector.scalar_tensor_tensor(out=xm[:, n % 2, c, :], in0=xx[:, c, :],
                                                              scalar=G.pv[:, col:col + 1], in1=xn[:, c, :],
                                                              op0=ALU.mult, op1=ALU.add)
                    last.then_inc(mixed, 1)

            @block.tensor
            def _(pe):
                g = [0]

                def group():
                    if g[0] >= 8:
                        pe.wait_ge(evac, g[0] - 7)
                    g[0] += 1
                    return bank[(g[0] - 1) % 8]

                def first(n, name, lo, m):
                    b = group()
                    for c in range(DC):
                        last = nc.tensor.matmul(b[0:m, 0:NT], w1[name][:, c, lo:lo + m], xm[:, n % 2, c, :],
                                                start=(c == 0), stop=(c == DC - 1))
                    last.then_inc(done, 1)

                pe.wait_ge(small_in, 7 * 16)
                pe.wait_ge(cols, 1)
                for half in range(2):
                    b = group()
                    for c in range(4):
                        last = nc.tensor.transpose(b[0:9, P * c:P * c + P], lastrow[:, 4 * half + c, :], G.ident[:, :])
                    last.then_inc(done, 1)
                for n, name in enumerate(("w", "a", "g")):
                    pe.wait_ge(mixed, n + 1)
                    if name == "g":
                        first(n, name, 0, P)
                        first(n, name, P, 32)
                    else:
                        first(n, name, 0, 64)
                    pe.wait_ge(evac, READ[name])
                    for c in range(DC):
                        b = group()
                        if name == "g":
                            nc.tensor.matmul(b[:, 0:NT], w2["g"][:, P * c:P * c + P], mid[:, 2, :], start=True, stop=False)
                            last = nc.tensor.matmul(b[:, 0:NT], g2b[:, P * c:P * c + P], mid[0:32, 3, :],
                                                    start=False, stop=True)
                        else:
                            last = nc.tensor.matmul(b[:, 0:NT], w2[name][:, P * c:P * c + P], mid[0:64, n, :],
                                                    start=True, stop=True)
                        last.then_inc(done, 1)
                for n, name in ((3, "r"), (4, "k"), (5, "v")):
                    pe.wait_ge(mixed, n + 1)
                    pe.wait_ge(rkv_in[(n - 3) % 2], 16 * (1 + (n == 5)))
                    for c in range(DC):
                        b = group()
                        for k in range(DC):
                            last = nc.tensor.matmul(b[:, 0:NT], big[:, (n - 3) % 2, k, P * c:P * c + P],
                                                    xm[:, n % 2, k, :], start=(k == 0), stop=(k == DC - 1))
                        last.then_inc(done, 1)

            @block.scalar
            def _(act):
                g = [0]

                def group():
                    g[0] += 1
                    act.wait_ge(done, g[0])
                    return bank[(g[0] - 1) % 8]

                for half in range(2):
                    b = group()
                    nc.scalar.copy(shrows[:, 512 * half:512 * half + 512], b[0:9, :]).then_inc(evac, 1)
                for n, (name, f, dst) in enumerate((("w", ACT.Tanh, R.sg), ("a", ACT.Copy, R.a), ("g", ACT.Sigmoid, R.g))):
                    for q in range(1 + (name == "g")):
                        m = 64 if name != "g" else (P, 32)[q]
                        b = group()
                        nc.scalar.activation(mid[0:m, n + q, :], b[0:m, 0:NT], f).then_inc(evac, 1)
                    for c in range(DC):
                        b = group()
                        if name == "g":
                            nc.scalar.copy(dst[:, c, :], b[:, 0:NT]).then_inc(evac, 1)
                        else:
                            col = (V_W0 if name == "w" else V_A0) + c
                            nc.scalar.activation(dst[:, c, :], b[:, 0:NT], ACT.Sigmoid,
                                                 bias=G.pv[:, col:col + 1]).then_inc(evac, 1)
                for name, dst in (("r", R.r), ("k", R.k), ("v", R.v)):
                    for c in range(DC):
                        b = group()
                        nc.scalar.copy(dst[:, c, :], b[:, 0:NT]).then_inc(evac, 1)


def per_feature(G, col, n):
    return G.pv[:, col:col + DC].unsqueeze(2).to_broadcast([P, DC, n])


def stage_derive(nc, G, R, W):
    with Scope(nc, "der") as s:
        X = s.sb("work", [P, 4, DC, NT])
        kk, b = s.sb("kk", [P, DC, NT]), s.sb("b", [P, DC, NT])
        one_ka = s.sb("one_minus_ka", [P, DC])
        hs = s.sb("head_sums", [NH, 3, NT])
        x1, x2, x3, x4 = (X[:, i] for i in range(4))
        rows = X[0:NS].rearrange("p a c t -> p (a c t)")[:, 0:6 * D].rearrange("p (i d) -> p i d", i=6)
        bank = [s.bank(f"b{i}") for i in range(8)]
        dchain, kk_raw, sq_ready, rk_ready = s.sem("dve_step"), s.sem("kk_raw"), s.sem("sq_ready"), s.sem("rk_ready")
        sums, clamped, rooted, inv = s.sem("sums"), s.sem("clamped"), s.sem("rooted"), s.sem("inverted")
        done, evac = s.sem("group_done"), s.sem("group_copied")
        summed, diffd, exp1, exp2, exp3, expd = (s.sem(n) for n in ("cumulated", "cum_before", "exp1", "exp2", "exp3", "decay"))
        scaled, spread = s.sem("scaled"), s.sem("samples_spread")
        NV = NP // CH
        with nc.Block() as block:
            @block.vector
            def _(dve):
                step = Chain(dve, dchain)
                nc.vector.tensor_tensor(kk[:, :, :], R.k[:, :, :], per_feature(G, V_KK, NT), ALU.mult).then_inc(kk_raw, 1)
                step(nc.vector.tensor_scalar(one_ka[:, :], G.pv[:, V_KA:V_KA + DC], -1.0, 1.0, ALU.mult, ALU.add))
                for c in range(DC):
                    last = nc.vector.tensor_scalar(x1[:, c, :], R.a[:, c, :], G.pv[:, V_KA + c:V_KA + c + 1],
                                                   one_ka[:, c:c + 1], ALU.mult, ALU.add)
                step(last)
                dve.wait_ge(kk_raw, 1)
                step(nc.vector.tensor_tensor(R.k[:, :, :], R.k[:, :, :], x1, ALU.mult))
                for c in range(DC):
                    last = nc.vector.scalar_tensor_tensor(out=x2[:, c, :], in0=R.r[:, c, :],
                                                          scalar=G.pv[:, V_RK + c:V_RK + c + 1], in1=R.k[:, c, :],
                                                          op0=ALU.mult, op1=ALU.mult)
                last.then_inc(rk_ready, 1)
                for c in range(DC):
                    for j in range(NV):
                        sl = slice(CH * j, CH * j + CH)
                        last = nc.vector.tensor_tensor_scan(x3[:, c, sl], G.ones[:, 0:CH], R.sg[:, c, sl], 0.0,
                                                            ALU.mult, ALU.add)
                last.then_inc(summed, 1)
                dve.wait_ge(summed, 1)
                nc.vector.tensor_tensor(x4[:, :, 0:NP], x3[:, :, 0:NP], R.sg[:, :, 0:NP], ALU.subtract).then_inc(diffd, 1)
                dve.wait_ge(sums, 2)
                nc.vector.tensor_scalar(hs[:, 0, :], bank[0][0:NH, 0:NT], 1e-24, None, ALU.max).then_inc(clamped, 1)
                nc.vector.tensor_copy(hs[:, 2, :], bank[1][0:NH, 0:NT])
                dve.wait_ge(rooted, 1)
                nc.vector.reciprocal(hs[:, 1, :], hs[:, 0, :]).then_inc(inv, 1)
                for c in range(DC):
                    dve.wait_ge(done, 2 * c + 1)
                    nc.vector.tensor_tensor(kk[:, c, :], kk[:, c, :], bank[(2 * c + 2) % 8][:, 0:NT], ALU.mult).then_inc(evac, 1)
                    dve.wait_ge(done, 2 * c + 2)
                    nc.vector.tensor_tensor(W.bonus[:, c, :], R.v[:, c, :], bank[(2 * c + 3) % 8][:, 0:NT],
                                            ALU.mult).then_inc(evac, 1)
                dve.wait_ge(evac, 16)
                step(nc.vector.tensor_tensor(b[:, :, :], kk[:, :, :], R.a[:, :, :], ALU.mult))
                dve.wait_ge(exp1, 1)
                nc.vector.tensor_copy(W.wc[:, :, :], x1[:, :, CH - 1:NP:CH])
                nc.vector.tensor_tensor(W.ar[:, :, 1, :], R.r[:, :, 0:NP], x1[:, :, 0:NP], ALU.mult)
                dve.wait_ge(exp2, 1)
                nc.vector.scalar_tensor_tensor(out=W.ar[:, :, 0, :], in0=kk[:, :, 0:NP], scalar=-1.0, in1=x4[:, :, 0:NP],
                                               op0=ALU.mult, op1=ALU.mult)
                dve.wait_ge(exp3, 1)
                nc.vector.tensor_tensor(W.bt[:, :, :], b[:, :, 0:NP], x2[:, :, 0:NP], ALU.mult)
                step(nc.vector.tensor_tensor(W.kt[:, :, :], R.k[:, :, 0:NP], x2[:, :, 0:NP], ALU.mult))
                for c in range(DC):
                    wc = W.wc[:, c, :].unsqueeze(2).to_broadcast([P, NV, CH])
                    ch = lambda t: t[:, c, 0:NP].rearrange("p (j t) -> p j t", t=CH)
                    nc.vector.tensor_tensor(ch(x1), ch(W.bt), wc, ALU.mult)
                    last = nc.vector.tensor_tensor(ch(x4), ch(W.kt), wc, ALU.mult)
                last.then_inc(scaled, 1)

            @block.scalar
            def _(act):
                act.wait_ge(kk_raw, 1)
                act.wait_ge(rk_ready, 1)
                nc.scalar.activation(x1, kk[:, :, :], ACT.Square).then_inc(sq_ready, 1)
                act.wait_ge(clamped, 1)
                nc.scalar.activation(hs[:, 0, :], hs[:, 0, :], ACT.Sqrt).then_inc(rooted, 1)
                act.wait_ge(diffd, 1)
                act.wait_ge(sums, 2)
                nc.scalar.activation(x1[:, :, 0:NP], x3[:, :, 0:NP], ACT.Exp, scale=-KAPPA).then_inc(exp1, 1)
                nc.scalar.activation(x4[:, :, 0:NP], x4[:, :, 0:NP], ACT.Exp, scale=-KAPPA).then_inc(exp2, 1)
                nc.scalar.activation(x2[:, :, 0:NP], x3[:, :, 0:NP], ACT.Exp, scale=KAPPA).then_inc(exp3, 1)
                nc.scalar.activation(R.sg[:, :, NP:NT], R.sg[:, :, NP:NT], ACT.Exp, scale=-KAPPA).then_inc(expd, 1)
                g = 16
                for dst in (W.vt, W.bht, W.kht):
                    for p in range(2):
                        for half in range(2):
                            g += 1
                            act.wait_ge(done, g)
                            nc.scalar.copy(dst[:, p, 512 * half:512 * half + 512], bank[(g + 1) % 8][:, :]).then_inc(evac, 1)
                for i in range(6):
                    for half in range(2):
                        g += 1
                        act.wait_ge(done, g)
                        nc.scalar.copy(rows[:, i, 512 * half:512 * half + 512], bank[(g + 1) % 8][0:NS, :]).then_inc(evac, 1)

            @block.tensor
            def _(pe):
                pe.wait_ge(sq_ready, 1)
                for c in range(DC):
                    last = nc.tensor.matmul(bank[0][0:NH, 0:NT], G.head_of[:, c, :], x1[:, c, :],
                                            start=(c == 0), stop=(c == DC - 1))
                last.then_inc(sums, 1)
                pe.wait_ge(rk_ready, 1)
                for c in range(DC):
                    last = nc.tensor.matmul(bank[1][0:NH, 0:NT], G.head_of[:, c, :], x2[:, c, :],
                                            start=(c == 0), stop=(c == DC - 1))
                last.then_inc(sums, 1)
                pe.wait_ge(inv, 1)
                g = 0
                for c in range(DC):
                    for i in (1, 2):
                        if g >= 6:
                            pe.wait_ge(evac, g - 5 if g < 8 else g - 7)
                        nc.tensor.matmul(bank[(g + 2) % 8][:, 0:NT], G.to_head[:, c, :], hs[:, i, :],
                                         start=True, stop=True).then_inc(done, 1)
                        g += 1
                pe.wait_ge(scaled, 1)
                for src in (R.v, x1, x4):
                    for p in range(2):
                        for half in range(2):
                            pe.wait_ge(evac, g - 7)
                            for c in range(4):
                                last = nc.tensor.transpose(bank[(g + 2) % 8][:, P * c:P * c + P],
                                                           src[:, 4 * half + c, P * p:P * p + P], G.ident[:, :])
                            last.then_inc(done, 1)
                            g += 1
                pe.wait_ge(expd, 1)
                for src in (R.r, R.sg, R.k, R.v, kk, b):
                    for half in range(2):
                        pe.wait_ge(evac, g - 7)
                        for c in range(4):
                            last = nc.tensor.transpose(bank[(g + 2) % 8][0:NS, P * c:P * c + P],
                                                       src[:, 4 * half + c, NP:NT], G.ident[:, :])
                        last.then_inc(done, 1)
                        g += 1

            @block.sync
            def _(sp):
                for i in range(6):
                    sp.wait_ge(evac, 28 + 2 * i + 2)
                    for t in range(DS):
                        sp.dma_start(W.sv[:, i, t, :], rows[t:NS:DS, i, :].rearrange("b (h d) -> b h d", d=HD)) \
                            .then_inc(spread, 16)
                sp.wait_ge(spread, 16 * 24)


def stage_wkv(nc, G, R, W, io, outer):
    W.y, W.ys = outer.sb("y", [P, 2, D]), outer.sb("y_sample", [P, DS, HD])
    with Scope(nc, "wkv") as s:
        akt, rkt, rbt, tt = (s.sb(n, [P, NH, P]) for n in ("ak", "rk", "rb", "inv_t"))
        lt, T, U, ltm = (s.sb(n, [P, 2, 4, P]) for n in ("l_t", "inv", "u", "l_level"))
        S0, S1 = s.sb("state", [P, DC, HD]), s.sb("state_decayed", [P, DC, HD])
        xs, sas = s.sb("x", [P, D]), s.sb("sa", [P, D])
        Ss, tmp = s.sb("state_sample", [P, HD, HD]), s.sb("outer", [P, HD // 2, HD])
        sav = s.sb("sa_sample", [P, HD // 2])
        so = xs[0:HD, :]
        bank = [s.bank(f"b{i}") for i in range(8)]
        pair_mm, pair_ev, ready = s.sem("pair_products"), s.sem("pair_masked"), s.sem("level_ready")
        u_mm, u_ev, d_mm = s.sem("u_products"), s.sem("u_copied"), s.sem("d_products")
        x_mm, x_ev, sa_mm, sa_ev = s.sem("x_products"), s.sem("x_copied"), s.sem("sa_products"), s.sem("sa_copied")
        y_mm, y_ev, s_mm, s_ev = s.sem("y_products"), s.sem("y_copied"), s.sem("state_products"), s.sem("state_ready")
        dchain, pchain, cleared = s.sem("dve_step"), s.sem("pool_step"), s.sem("cleared")
        st_mm, st_ev, st_in, st_out = s.sem("state_turned"), s.sem("state_copied"), s.sem("state_in"), s.sem("state_out")
        steps_done = s.sem("sample_steps_done")
        tile = lambda p: slice(P * p, P * p + P)
        with nc.Block() as block:
            @block.tensor
            def _(pe):
                for p in range(2):
                    for half in range(2):
                        for i in range(4):
                            n = 8 * p + 4 * half + i
                            if i < 2 and n >= 4:
                                pe.wait_ge(ready, 12 * (2 * p + half))
                            if i < 2 and half == 0 and p == 1:
                                pe.wait_ge(y_ev, 2)
                                pe.wait_ge(s_ev, 3)
                            if i >= 2:
                                pe.wait_ge(pair_ev, n - 1)
                            for q in range(2):
                                b, b2 = bank[4 * (i % 2) + q], bank[4 * (i % 2) + 2 + q]
                                c, hb = (8 * half + 2 * i + q) // 2, HD * q
                                f = slice(hb, hb + HD)
                                rhs = W.ar[f, c, :, tile(p)]
                                nc.tensor.matmul(b[:, 0:256], W.kt[f, c, tile(p)], rhs, start=True, stop=True)
                                nc.tensor.matmul(b[:, 256:512], W.bt[f, c, tile(p)], rhs, start=True, stop=True)
                                last = nc.tensor.matmul(b2[:, 0:P], W.ar[f, c, 0, tile(p)],
                                                        W.bt[f, c, tile(p)], start=True, stop=True)
                            last.then_inc(pair_mm, 1)
                        for l in range(1, 6):
                            n = 12 * (2 * p + half) + 2 * (l - 1)
                            m = 10 * (2 * p + half) + 2 * (l - 1)
                            for st in range(2):
                                pe.wait_ge(ready, n + st + 1)
                                for h in range(4):
                                    last = nc.tensor.matmul(bank[st][:, P * h:P * h + P], ltm[:, st, h, :], T[:, st, h, :],
                                                            start=True, stop=True)
                                last.then_inc(u_mm, 1)
                            for st in range(2):
                                pe.wait_ge(u_ev, m + st + 1)
                                for h in range(4):
                                    hh = 8 * half + 4 * st + h
                                    if l < 5:
                                        nc.tensor.matmul(bank[2 + st][:, P * h:P * h + P], tt[:, hh, :], U[:, st, h, :],
                                                         start=True, stop=True)
                                    last = nc.tensor.matmul(bank[4 + st][:, P * h:P * h + P], U[:, st, h, :], tt[:, hh, :],
                                                            start=True, stop=True)
                                last.then_inc(d_mm, 1)
                    pe.wait_ge(ready, 24 * (p + 1))
                    pe.wait_ge(cleared, 1)
                    for j in range(2):
                        ch = 2 * p + j
                        rows = slice(CH * j, CH * j + CH)
                        pe.wait_ge(s_ev, ch + 1)
                        for h in range(NH):
                            c, f = h // 2, slice(HD * (h % 2), HD * (h % 2) + HD)
                            o = bank[h % 2][:, HD * c:HD * c + HD]
                            nc.tensor.matmul(o, W.ar[f, c, 0, tile(p)], S0[f, c, :], start=True, stop=False)
                            last = nc.tensor.matmul(o, akt[:, h, :], W.vt[:, p, HD * h:HD * h + HD], start=False, stop=True)
                        last.then_inc(x_mm, 1)
                        pe.wait_ge(x_ev, ch + 1)
                        for h in range(NH):
                            last = nc.tensor.matmul(bank[2 + h % 2][:, HD * (h // 2):HD * (h // 2) + HD], tt[:, h, :],
                                                    xs[:, HD * h:HD * h + HD], start=True, stop=True)
                        last.then_inc(sa_mm, 1)
                        pe.wait_ge(sa_ev, ch + 1)
                        for c in range(DC):
                            o = bank[6 + c // 4][:, P * (c % 4):P * (c % 4) + P]
                            col = slice(P * c, P * c + P)
                            nc.tensor.matmul(o, W.bht[rows, p, col], sas[rows, col], start=True, stop=False)
                            nc.tensor.matmul(o, W.kht[rows, p, col], W.vt[rows, p, col], start=False, stop=True)
                        for h in range(NH):
                            c, f = h // 2, slice(HD * (h % 2), HD * (h % 2) + HD)
                            o = bank[4 + h % 2][:, HD * c:HD * c + HD]
                            hc = slice(HD * h, HD * h + HD)
                            nc.tensor.matmul(o, W.ar[f, c, 1, tile(p)], S0[f, c, :], start=True, stop=False)
                            nc.tensor.matmul(o, rbt[:, h, :], sas[:, hc], start=False, stop=False)
                            last = nc.tensor.matmul(o, rkt[:, h, :], W.vt[:, p, hc], start=False, stop=True)
                        last.then_inc(y_mm, 1)
                pe.wait_ge(s_ev, 5)
                for c in range(DC):
                    last = nc.tensor.transpose(bank[c // 4][0:HD, P * (c % 4):P * (c % 4) + P], S0[:, c, :], G.ident[:, :])
                last.then_inc(st_mm, 1)

            @block.vector
            def _(dve):
                step = Chain(dve, dchain)
                nc.vector.memset(xs[:, :], 0.0)
                nc.vector.memset(sas[:, :], 0.0).then_inc(cleared, 1)
                nc.vector.memset(S0[:, :, :], 0.0).then_inc(s_ev, 1)
                dve.wait_ge(s_ev, 1)
                four = lambda m: m.unsqueeze(1).to_broadcast([P, 4, P])
                for p in range(2):
                    for half in range(2):
                        for i in range(4):
                            n = 8 * p + 4 * half + i
                            dve.wait_ge(pair_mm, n + 1)
                            if n == 8:
                                dve.wait_ge(y_mm, 2)
                            st = i // 2
                            for q in range(2):
                                b, b2 = bank[4 * (i % 2) + q], bank[4 * (i % 2) + 2 + q]
                                h, hq = 8 * half + 2 * i + q, 2 * (i % 2) + q
                                nc.vector.tensor_tensor(akt[:, h, :], b[:, 0:P], G.mask_su[:, :], ALU.mult)
                                nc.vector.tensor_tensor(rkt[:, h, :], b[:, P:2 * P], G.mask_iu[:, :], ALU.mult)
                                nc.vector.tensor_tensor(lt[:, st, hq, :], b[:, 2 * P:3 * P], G.mask_su[:, :], ALU.mult)
                                nc.vector.tensor_tensor(rbt[:, h, :], b[:, 3 * P:4 * P], G.mask_iu[:, :], ALU.mult)
                                last = nc.vector.tensor_tensor(T[:, st, hq, :], b2[:, 0:P], G.level[:, 7, :], ALU.mult)
                            last.then_inc(pair_ev, 1)
                        dve.wait_ge(pair_ev, 4 * (2 * p + half) + 4)
                        for st in range(2):
                            hs = slice(8 * half + 4 * st, 8 * half + 4 * st + 4)
                            step(nc.vector.tensor_tensor(tt[:, hs, :], lt[:, st], four(G.level[:, 0, :]), ALU.mult))
                            nc.vector.tensor_tensor(T[:, st], T[:, st], four(G.ident[:, :]), ALU.add)
                            nc.vector.tensor_tensor(tt[:, hs, :], tt[:, hs, :], four(G.ident[:, :]), ALU.add)
                            nc.vector.tensor_tensor(ltm[:, st], lt[:, st], four(G.level[:, 1, :]), ALU.mult).then_inc(ready, 1)
                        for l in range(1, 6):
                            for st in range(2):
                                hs = slice(8 * half + 4 * st, 8 * half + 4 * st + 4)
                                dve.wait_ge(ready, 12 * (2 * p + half) + 2 * (l - 1) + st + 1)
                                dve.wait_ge(d_mm, 10 * (2 * p + half) + 2 * (l - 1) + st + 1)
                                view = lambda b: b[:, :].rearrange("p (h t) -> p h t", h=4)
                                if l < 5:
                                    nc.vector.tensor_tensor(T[:, st], T[:, st], view(bank[2 + st]), ALU.add)
                                last = nc.vector.tensor_tensor(tt[:, hs, :], tt[:, hs, :], view(bank[4 + st]), ALU.add)
                                if l < 5:
                                    last = nc.vector.tensor_tensor(ltm[:, st], lt[:, st], four(G.level[:, l + 1, :]), ALU.mult)
                                last.then_inc(ready, 1)
                    for j in range(2):
                        ch = 2 * p + j
                        wc = W.wc[:, :, ch].unsqueeze(2).to_broadcast([P, DC, HD])
                        step(nc.vector.tensor_tensor(S1[:, :, :], S0[:, :, :], wc, ALU.mult))
                        dve.wait_ge(y_mm, ch + 1)
                        for half in range(2):
                            cs = slice(4 * half, 4 * half + 4)
                            pv = bank[6 + half][:, :].rearrange("p (c x v) -> p c x v", c=4, x=2)
                            for q in range(2):
                                f = slice(HD * q, HD * q + HD)
                                last = nc.vector.tensor_tensor(S0[f, cs, :], S1[f, cs, :], pv[f, :, q, :], ALU.add)
                        last.then_inc(s_ev, 1)
                        dve.wait_ge(s_ev, ch + 2)

            @block.scalar
            def _(act):
                for p in range(2):
                    for half in range(2):
                        for l in range(1, 6):
                            for st in range(2):
                                n = 10 * (2 * p + half) + 2 * (l - 1) + st
                                act.wait_ge(u_mm, n + 1)
                                nc.scalar.copy(U[:, st].rearrange("p h t -> p (h t)"), bank[st][:, :]).then_inc(u_ev, 1)
                    act.wait_ge(cleared, 1)
                    for j in range(2):
                        ch = 2 * p + j
                        rows = slice(CH * j, CH * j + CH)
                        for mm, ev, dst, b in ((x_mm, x_ev, xs, 0), (sa_mm, sa_ev, sas, 2), (y_mm, y_ev, W.y[:, p, :], 4)):
                            act.wait_ge(mm, ch + 1)
                            by_parity = dst[rows, :].rearrange("p (c q v) -> p c q v", q=2, v=HD)
                            for q in range(2):
                                last = nc.scalar.copy(by_parity[:, :, q, :],
                                                      bank[b + q][rows, :].rearrange("p (c v) -> p c v", v=HD))
                            last.then_inc(ev, 1)
                act.wait_ge(st_mm, 1)
                for half in range(2):
                    nc.scalar.copy(so[:, 512 * half:512 * half + 512], bank[half][0:HD, :]).then_inc(st_ev, 1)

            @block.gpsimd
            def _(pool):
                step = Chain(pool, pchain)
                over_k = lambda i, t: W.sv[:, i, t, :].unsqueeze(1).to_broadcast([P, HD // 2, HD])
                over_v = lambda ap: ap.unsqueeze(2).to_broadcast([P, HD // 2, HD])
                tt_ = nc.gpsimd.tensor_tensor

                def sum_k(dst):
                    n = HD // 2
                    while n > 1:
                        step(tt_(tmp[:, :, 0:n], tmp[:, :, 0:n], tmp[:, :, n:2 * n], ALU.add))
                        n //= 2
                    step(tt_(dst, tmp[:, :, 0], tmp[:, :, 1], ALU.add))

                pool.wait_ge(st_in, 16)
                for t in range(DS):
                    for half in range(2):
                        vs = slice(HD // 2 * half, HD // 2 * half + HD // 2)
                        S = Ss[:, vs, :]
                        step(tt_(tmp[:, :, :], S, over_k(4, t), ALU.mult))
                        sum_k(sav[:, :])
                        step(tt_(S, S, over_k(1, t), ALU.mult))
                        step(tt_(tmp[:, :, :], over_v(sav[:, :]), over_k(5, t), ALU.mult))
                        step(tt_(S, S, tmp[:, :, :], ALU.subtract))
                        step(tt_(tmp[:, :, :], over_v(W.sv[:, 3, t, vs]), over_k(2, t), ALU.mult))
                        step(tt_(S, S, tmp[:, :, :], ALU.add))
                        step(tt_(tmp[:, :, :], S, over_k(0, t), ALU.mult))
                        sum_k(W.ys[:, t, vs])
                pool.sem_inc(steps_done, 1)

            @block.sync
            def _(sp):
                sp.dma_start(Ss[:, :, :], io["state_wkv"][0].rearrange("b h v k -> (b h) v k")).then_inc(st_in, 16)
                sp.wait_ge(st_ev, 2)
                sp.dma_start(io["wkv_prompt"][0, 0].rearrange("h v k -> v h k"),
                             so.rearrange("v (h k) -> v h k", k=HD)).then_inc(st_out, 16)
                sp.wait_ge(steps_done, 1)
                sp.dma_start(io["wkv_sample"][0].rearrange("b h v k -> (b h) v k"), Ss[:, :, :]).then_inc(st_out, 16)
                sp.wait_ge(st_out, 32)


def stage_rwkv_out(nc, G, R, W, io):
    with Scope(nc, "rout") as s:
        wo = s.sb("wo", [P, DC, D])
        ysq, yq = s.sb("y_sq", [P, 2 * NH + DS, HD]), s.sb("stats", [P, 4, 2 * NH + DS])
        rows, z = s.sb("y_rows", [NS, D]), s.sb("z", [P, DC, NT])
        bank = [s.bank(f"b{i}") for i in range(8)]
        wo_in, dchain, centred, squared = s.sem("wo_in"), s.sem("dve_step"), s.sem("centred"), s.sem("squared")
        var, rooted, normed, spread = s.sem("var"), s.sem("rooted"), s.sem("normed"), s.sem("rows_in")
        turned, zr, mm, ev = s.sem("turned"), s.sem("z_ready"), s.sem("products"), s.sem("added")
        y3 = W.y[:, :, :].rearrange("p a (h d) -> p (a h) d", d=HD)
        n1 = 2 * NH
        with nc.Block() as block:
            @block.sync
            def _(sp):
                sp.dma_start(wo[:, :, :], io["rw_w_o"][0].rearrange("(c p) n -> p c n", p=P)).then_inc(wo_in, 16)
                sp.wait_ge(normed, 1)
                for t in range(DS):
                    sp.dma_start(rows[t:NS:DS, :].rearrange("b (h d) -> b h d", d=HD), W.ys[:, t, :]).then_inc(spread, 16)

            @block.vector
            def _(dve):
                step = Chain(dve, dchain)
                nc.vector.reduce_sum(yq[:, 0, 0:n1], y3, axis=AX)
                step(nc.vector.reduce_sum(yq[:, 0, n1:], W.ys[:, :, :], axis=AX))
                step(nc.vector.tensor_scalar(yq[:, 1, :], yq[:, 0, :], 1.0 / HD, None, ALU.mult))
                nc.vector.tensor_tensor(y3, y3, yq[:, 1, 0:n1].unsqueeze(2).to_broadcast([P, n1, HD]), ALU.subtract)
                nc.vector.tensor_tensor(W.ys[:, :, :], W.ys[:, :, :], yq[:, 1, n1:].unsqueeze(2).to_broadcast([P, DS, HD]),
                                        ALU.subtract).then_inc(centred, 1)
                dve.wait_ge(squared, 1)
                nc.vector.reduce_sum(yq[:, 2, :], ysq[:, :, :], axis=AX).then_inc(var, 1)
                dve.wait_ge(rooted, 1)
                step(nc.vector.reciprocal(yq[:, 0, :], yq[:, 3, :]))
                nc.vector.tensor_tensor(y3, y3, yq[:, 0, 0:n1].unsqueeze(2).to_broadcast([P, n1, HD]), ALU.mult)
                nc.vector.tensor_tensor(W.ys[:, :, :], W.ys[:, :, :], yq[:, 0, n1:].unsqueeze(2).to_broadcast([P, DS, HD]),
                                        ALU.mult).then_inc(normed, 1)
                for n in range(5):
                    dve.wait_ge(turned, n + 1)
                    for c in range(4 if n < 4 else DC):
                        cc, p = (4 * (n % 2) + c, n // 2) if n < 4 else (c, 2)
                        w = P if n < 4 else NS
                        last = nc.vector.tensor_scalar(z[:, cc, P * p:P * p + w], bank[n][:, w * c:w * c + w],
                                                       G.pv[:, V_LNW + cc:V_LNW + cc + 1], G.pv[:, V_LNB + cc:V_LNB + cc + 1],
                                                       ALU.mult, ALU.add)
                step(last)
                step(nc.vector.tensor_tensor(z[:, :, :], z[:, :, :], W.bonus[:, :, :], ALU.add))
                nc.vector.tensor_tensor(z[:, :, :], z[:, :, :], R.g[:, :, :], ALU.mult).then_inc(zr, 1)
                for c in range(DC):
                    dve.wait_ge(mm, c + 1)
                    nc.vector.tensor_tensor(G.h[:, c, :], G.h[:, c, :], bank[c % 8][:, 0:NT], ALU.add).then_inc(ev, 1)

            @block.scalar
            def _(act):
                act.wait_ge(centred, 1)
                nc.scalar.activation(ysq[:, 0:n1, :], y3, ACT.Square)
                nc.scalar.activation(ysq[:, n1:, :], W.ys[:, :, :], ACT.Square).then_inc(squared, 1)
                act.wait_ge(var, 1)
                nc.scalar.activation(yq[:, 3, :], yq[:, 2, :], ACT.Sqrt, scale=1.0 / HD, bias=G.gneps[:, 0:1]).then_inc(rooted, 1)

            @block.tensor
            def _(pe):
                pe.wait_ge(normed, 1)
                for n in range(4):
                    for c in range(4):
                        cc = 4 * (n % 2) + c
                        last = nc.tensor.transpose(bank[n][:, P * c:P * c + P], W.y[:, n // 2, P * cc:P * cc + P], G.ident[:, :])
                    last.then_inc(turned, 1)
                pe.wait_ge(spread, 16 * DS)
                for c in range(DC):
                    last = nc.tensor.transpose(bank[4][:, NS * c:NS * c + NS], rows[:, P * c:P * c + P], G.ident[0:NS, 0:NS])
                last.then_inc(turned, 1)
                pe.wait_ge(zr, 1)
                pe.wait_ge(wo_in, 16)
                for c in range(DC):
                    for k in range(DC):
                        last = nc.tensor.matmul(bank[c][:, 0:NT], wo[:, k, P * c:P * c + P], z[:, k, :],
                                                start=(k == 0), stop=(k == DC - 1))
                    last.then_inc(mm, 1)


GW = 256
NG = F_FF // GW


F32R = mybir.dt.float32r


def product(nc, out, w_hi, w_lo, x_hi, x_lo, start, stop):
    nc.tensor.matmul(out, w_hi, x_hi, start=start, stop=False)
    nc.tensor.matmul(out, w_hi, x_lo, start=False, stop=False)
    return nc.tensor.matmul(out, w_lo, x_hi, start=False, stop=stop)


def stage_ffn(nc, G, io):
    with Scope(nc, "ffn") as s:
        xn, xh, xl = s.sb("xn", [P, DC, NT]), s.sb("xn_hi", [P, DC, NT], F32R), s.sb("xn_lo", [P, DC, NT], F32R)
        RING, ROWS = 2, 4
        ND = -(-FC // ROWS)
        W = s.sb("w", [P, RING, 2 * DC * GW])
        WH, WL = (s.sb(n, [P, 2, 2 * DC * GW], F32R) for n in ("w_hi", "w_lo"))
        HH, HL = (s.sb(n, [P, FC, NT], F32R) for n in ("hidden_hi", "hidden_lo"))
        silu_b, H = s.sb("silu", [P, 2, NT]), s.sb("hidden", [P, 2, NT])
        bank = [s.bank(f"b{i}") for i in range(8)]
        w_in = [s.sem(f"w_in{i}") for i in range(RING)]
        xhi, xlo, high, ready, used = (s.sem(n) for n in ("x_high", "x_low", "w_high", "w_ready", "down_groups_used"))
        mm, silu, raw, hhi, hid, down, added = (s.sem(n) for n in (
            "products", "silu", "hidden_raw", "hidden_high", "hidden", "down", "added"))
        count = lambda j: FC - ROWS * j if j == ND - 1 else ROWS
        size = lambda n: 2 * DC * GW if n < NG else count(n - NG) * D

        def wait_used(eng, n):
            if 2 <= n < NG + 2:
                eng.wait_ge(mm, 2 * (n - 2) + 2)
            elif n >= NG + 2:
                eng.wait_ge(used, n - NG - 1)

        def load(sp, n):
            slot, sem = W[:, n % RING, 0:size(n)], w_in[n % RING]
            if n < NG:
                for i, name in enumerate(("ffn_w_gate", "ffn_w_up")):
                    sp.dma_start(slot.rearrange("p (x k n) -> p x k n", x=2, k=DC)[:, i],
                                 io[name][0, :, GW * n:GW * n + GW].rearrange("(k p) n -> p k n", p=P)).then_inc(sem, 16)
            else:
                r = P * ROWS * (n - NG)
                for i in range(2):
                    h = count(n - NG) // 2
                    sp.dma_start(slot.rearrange("p (k n) -> p k n", n=D)[:, h * i:h * i + h],
                                 io["ffn_w_down"][0, r + P * h * i:r + P * h * i + P * h, :].rearrange("(k p) n -> p k n", p=P)) \
                        .then_inc(sem, 16)

        stage_norm(nc, G, "norm1", C_NG + 8, xn, lambda sp: [load(sp, n) for n in range(RING)], H, bank[0])
        with nc.Block() as block:
            @block.sync
            def _(sp):
                for n in range(RING, NG + ND):
                    sp.wait_ge(ready, n - RING + 1)
                    load(sp, n)

            @block.tensor
            def _(pe):
                pe.wait_ge(xlo, 1)
                for f in range(FC):
                    n = f // 2
                    if f % 2 == 0:
                        pe.wait_ge(ready, n + 1)
                    if f >= 4:
                        pe.wait_ge(raw, f - 3)
                    hi, lo = (t.rearrange("p (x k n) -> p x k n", x=2, k=DC) for t in (WH[:, n % 2], WL[:, n % 2]))
                    for x in range(2):
                        for k in range(DC):
                            cols = slice(P * (f % 2), P * (f % 2) + P)
                            last = product(nc, bank[2 * (f % 4) + x][:, 0:NT], hi[:, x, k, cols], lo[:, x, k, cols],
                                           xh[:, k, :], xl[:, k, :], k == 0, k == DC - 1)
                    last.then_inc(mm, 1)
                pe.wait_ge(hid, FC)
                for j in range(ND):
                    n = NG + j
                    pe.wait_ge(ready, n + 1)
                    hi, lo = (t[:, 0:size(n)].rearrange("p (k n) -> p k n", n=D) for t in (WH[:, n % 2], WL[:, n % 2]))
                    for c in range(DC):
                        for k in range(count(j)):
                            f, cols = ROWS * j + k, slice(P * c, P * c + P)
                            last = product(nc, bank[c][:, 0:NT], hi[:, k, cols], lo[:, k, cols],
                                           HH[:, f, :], HL[:, f, :], f == 0, f == FC - 1)
                        if j == ND - 1:
                            last.then_inc(down, 1)
                    if j < ND - 1:
                        last.then_inc(used, 1)

            @block.scalar
            def _(act):
                def split(n):
                    act.wait_ge(w_in[n % RING], 32 * (n // RING + 1))
                    wait_used(act, n)
                    nc.scalar.copy(WH[:, n % 2, 0:size(n)], W[:, n % RING, 0:size(n)]).then_inc(high, 1)

                nc.scalar.copy(xh[:, :, :], xn[:, :, :]).then_inc(xhi, 1)
                split(0)
                split(1)
                for f in range(FC):
                    act.wait_ge(mm, f + 1)
                    if f >= 2:
                        act.wait_ge(raw, f - 1)
                    nc.scalar.activation(silu_b[:, f % 2, :], bank[2 * (f % 4)][:, 0:NT], ACT.Silu).then_inc(silu, 1)
                    if f:
                        act.wait_ge(raw, f)
                        nc.scalar.copy(HH[:, f - 1, :], H[:, (f - 1) % 2, :]).then_inc(hhi, 1)
                    if f % 2 == 1 and f < FC - 1:
                        split(f // 2 + 2)
                act.wait_ge(raw, FC)
                nc.scalar.copy(HH[:, FC - 1, :], H[:, (FC - 1) % 2, :]).then_inc(hhi, 1)
                for n in range(NG + 1, NG + ND):
                    split(n)

            @block.vector
            def _(dve):
                def low(n):
                    dve.wait_ge(high, n + 1)
                    w = W[:, n % RING, 0:size(n)]
                    wait_used(dve, n)
                    nc.vector.tensor_tensor(WL[:, n % 2, 0:size(n)], w, WH[:, n % 2, 0:size(n)], ALU.subtract).then_inc(ready, 1)

                def hidden_low(f):
                    dve.wait_ge(hhi, f + 1)
                    nc.vector.tensor_tensor(HL[:, f, :], H[:, f % 2, :], HH[:, f, :], ALU.subtract).then_inc(hid, 1)

                dve.wait_ge(xhi, 1)
                nc.vector.tensor_tensor(xl[:, :, :], xn[:, :, :], xh[:, :, :], ALU.subtract).then_inc(xlo, 1)
                low(0)
                low(1)
                for f in range(FC):
                    dve.wait_ge(silu, f + 1)
                    if f >= 2:
                        dve.wait_ge(hid, f - 1)
                    nc.vector.tensor_tensor(H[:, f % 2, :], silu_b[:, f % 2, :], bank[2 * (f % 4) + 1][:, 0:NT],
                                            ALU.mult).then_inc(raw, 1)
                    if f:
                        hidden_low(f - 1)
                    if f % 2 == 1 and f < FC - 1:
                        low(f // 2 + 2)
                hidden_low(FC - 1)
                for n in range(NG + 1, NG + ND):
                    low(n)
                for c in range(DC):
                    dve.wait_ge(down, c + 1)
                    nc.vector.tensor_tensor(G.h[:, c, :], G.h[:, c, :], bank[c][:, 0:NT], ALU.add).then_inc(added, 1)


KV = 3 * 2 * 2
KC = {"slc": (4, 5), "win": (8, 9)}


def stage_kv(nc, G, K, io):
    with Scope(nc, "kv") as s:
        xn = s.sb("xn", [P, DC, NT])
        w = s.sb("w", [P, DC, KV * P])
        kvt, sq = s.sb("kv_t", [P, KV, NT]), s.sb("sq", [P, 4, NT])
        hs, rows = s.sb("head_sums", [8, 2, NT]), s.sb("rows", [P, 3, 3 * 512])
        bank = [s.bank(f"b{i}") for i in range(8)]
        w_in = [s.sem(f"w_in{i}") for i in range(2)]
        mm, ev, sqr, ss, root, inv, spread, normed = (s.sem(n) for n in (
            "products", "copied", "squared", "sums", "rooted", "inverted", "spread", "normed"))
        turned, rows_ev, out, win_out = s.sem("turned"), s.sem("rows_copied"), s.sem("kv_out"), s.sem("win_out")
        ks = (4, 5, 8, 9)

        def ahead(sp):
            for i in range(2):
                sp.dma_start(w[:, 4 * i:4 * i + 4], io["w_kv"][P * 4 * i:P * 4 * i + 512, :].rearrange("(k p) n -> p k n", p=P)) \
                    .then_inc(w_in[i], 16)

        stage_norm(nc, G, "norm2", C_KVG, xn, ahead, kvt, bank[0])
        with nc.Block() as block:
            @block.sync
            def _(sp):
                sp.wait_ge(K.zeroed, 2)
                for g2 in range(2):
                    f = slice(HD * g2, HD * g2 + HD)
                    for x in range(2):
                        sp.dma_start(K.w1[f, x, :, f], io["cmp_w1"][x].rearrange("s d h -> d s h")).then_inc(K.cmp_in, 16)
                        sp.dma_start(K.w2[f, x, f], io["cmp_w2"][x]).then_inc(K.cmp_in, 16)
                    sp.dma_start(K.per[:, f], io["cmp_pe"].rearrange("x s d -> (x s) d")).then_inc(K.cmp_in, 16)
                sp.dma_start(io["win_kv_sample"][:, 0:512 - DS].rearrange("b r x g d -> b (r x g d)"),
                             io["state_win_kv"][:, DS:512].rearrange("b r x g d -> b (r x g d)")).then_inc(win_out, 16)
                sp.wait_ge(rows_ev, 9)
                for i, name in enumerate(("cmp", "slc", "win")):
                    col = slice(512 * i, 512 * i + 512)
                    sp.dma_start(io[f"{name}_kv_prompt"][0].rearrange("(n p) x g d -> p n (x g d)", p=P),
                                 rows[:, 0:2, col]).then_inc(out, 16)
                    if i < 2:
                        sp.dma_start(io[f"{name}_kv_sample"].rearrange("b t x g d -> (b t) (x g d)"),
                                     rows[0:NS, 2, col]).then_inc(out, 16)
                    else:
                        for b in range(NB):
                            sp.dma_start(io["win_kv_sample"][b, 512 - DS:512].rearrange("t x g d -> t (x g d)"),
                                         rows[DS * b:DS * b + DS, 2, col]).then_inc(out, 16)
                sp.wait_ge(out, 16 * (5 + NB))
                sp.wait_ge(win_out, 16)

            @block.tensor
            def _(pe):
                for j in range(KV):
                    if j >= 8:
                        pe.wait_ge(ev, j - 7)
                    for k in range(DC):
                        if j == 0 and k % 4 == 0:
                            pe.wait_ge(w_in[k // 4], 16)
                        last = nc.tensor.matmul(bank[j % 8][:, 0:NT], w[:, k, P * j:P * j + P], xn[:, k, :],
                                                start=(k == 0), stop=(k == DC - 1))
                    last.then_inc(mm, 1)
                pe.wait_ge(ev, KV)
                pe.wait_ge(sqr, 1)
                for i in range(4):
                    last = nc.tensor.matmul(bank[4][0:8, 0:NT], G.head_of[:, i, 0:8], sq[:, i, :], start=(i == 0), stop=(i == 3))
                last.then_inc(ss, 1)
                pe.wait_ge(inv, 1)
                for i in range(4):
                    nc.tensor.matmul(bank[i][:, 0:NT], G.to_head[0:8, i, :], hs[:, 1, :], start=True, stop=True).then_inc(spread, 1)
                pe.wait_ge(normed, 4)
                for n in range(9):
                    t, br = divmod(n, 3)
                    m = P if t < 2 else NS
                    if n >= 8:
                        pe.wait_ge(rows_ev, n - 7)
                    for i in range(4):
                        last = nc.tensor.transpose(bank[n % 8][0:m, P * i:P * i + P], kvt[:, 4 * br + i, P * t:P * t + m],
                                                   G.ident[:, :])
                    last.then_inc(turned, 1)

            @block.scalar
            def _(act):
                for j in range(KV):
                    act.wait_ge(mm, j + 1)
                    nc.scalar.copy(kvt[:, j, :], bank[j % 8][:, 0:NT]).then_inc(ev, 1)
                act.wait_ge(ev, KV)
                for i, j in enumerate(ks):
                    last = nc.scalar.activation(sq[:, i, :], kvt[:, j, :], ACT.Square)
                last.then_inc(sqr, 1)
                act.wait_ge(ss, 1)
                nc.scalar.activation(hs[:, 0, :], bank[4][0:8, 0:NT], ACT.Sqrt, scale=1.0 / HD,
                                     bias=G.eps[0:8, 0:1]).then_inc(root, 1)
                for n in range(9):
                    t, br = divmod(n, 3)
                    m = P if t < 2 else NS
                    act.wait_ge(turned, n + 1)
                    nc.scalar.copy(rows[0:m, t, 512 * br:512 * br + 512], bank[n % 8][0:m, :]).then_inc(rows_ev, 1)

            @block.vector
            def _(dve):
                nc.vector.memset(K.w1[:, :, :, :], 0.0).then_inc(K.zeroed, 1)
                nc.vector.memset(K.w2[:, :, :], 0.0).then_inc(K.zeroed, 1)
                dve.wait_ge(root, 1)
                nc.vector.reciprocal(hs[:, 1, :], hs[:, 0, :]).then_inc(inv, 1)
                for i, j in enumerate(ks):
                    dve.wait_ge(spread, i + 1)
                    br = j // 4
                    nc.vector.scalar_tensor_tensor(out=kvt[:, j, :], in0=kvt[:, j, :], scalar=G.pv[:, C_KN + br:C_KN + br + 1],
                                                   in1=bank[i][:, 0:NT], op0=ALU.mult, op1=ALU.mult).then_inc(normed, 1)
                dve.wait_ge(normed, 4)
                for i, j in enumerate(ks):
                    last = nc.vector.tensor_copy(K.kt[:, i, :], kvt[:, j, :])
                dve.wait_ge(rows_ev, 9)
                for t in range(3):
                    m = P if t < 2 else NS
                    for br in range(2):
                        nc.vector.tensor_copy(K.vn[0:m, t, br, :], rows[0:m, t, 512 * (br + 1) + 256:512 * (br + 1) + 512])


PAST, PAGE = 2048, 128
SUB = 16
NSUB = PAST // SUB
NCMP = NSUB - 1
NSUB_P = NP // SUB
NCMP_P = NSUB_P - 1
RW = SUB * 512
NSEQ = NB + 1


def stage_index(nc, G, K, io):
    with Scope(nc, "idx") as s:
        pages, part = s.sb("pages", [P, NB], I32), s.sb("part", [P, 1], I32)
        pages_in, made, low = s.sem("pages_in"), s.sem("made"), s.sem("low_bits")
        per = PAGE // SUB
        with nc.Block() as block:
            @block.sync
            def _(sp):
                for q in range(per):
                    sp.dma_start(pages[q:P:per, :], io["page_table"].rearrange("b n -> n b"),
                                 allow_slow_non_contiguous=True).then_inc(pages_in, 16)

            @block.gpsimd
            def _(pool):
                nc.gpsimd.iota(part[:, :], pattern=[[0, 1]], base=0, channel_multiplier=1).then_inc(made, 1)

            @block.vector
            def _(dve):
                dve.wait_ge(made, 1)
                nc.vector.tensor_single_scalar(part[:, :], part[:, :], per - 1, ALU.bitwise_and).then_inc(low, 1)
                dve.wait_ge(low, 1)
                dve.wait_ge(pages_in, 16 * per)
                nc.vector.tensor_scalar(K.idx[:, :], pages[:, :], per, None, ALU.mult).then_inc(low, 1)
                dve.wait_ge(low, 2)
                nc.vector.tensor_tensor(K.idx[:, :], K.idx[:, :], part[:, :].to_broadcast([P, NB]), ALU.add)


def stage_compress(nc, G, K, io):
    with Scope(nc, "cmp") as s:
        Z = s.sb("rows", [P, 2, RW])
        XT = s.sb("rows_t", [P, 2, SUB, 2, P])
        w1, w2, per = K.w1, K.w2, K.per
        pet, bias = s.sb("pe_t", [P, 4 * SUB]), s.sb("bias", [P, 2])
        sl, kraw, sq = s.sb("silu", [P, 2, 2, NCMP]), s.sb("k_raw", [P, 2 * NCMP]), s.sb("sq", [P, 2 * NCMP])
        std, rstd = s.sb("std", [P, 2 * NCMP]), s.sb("rstd", [P, 2 * NCMP])
        bank = [s.bank(f"b{i}") for i in range(8)]
        z_in = [s.sem(f"rows_in{i}") for i in range(2)]
        zp_in = s.sem("prompt_rows_in")
        setup, biased = s.sem("setup"), s.sem("biased")
        turned, ev_a, ev_v = s.sem("turned"), s.sem("copied_act"), s.sem("copied_dve")
        pre, silu, k_mm, k_ev, ss, root, rt, kc, v_mm, v_ev = (s.sem(n) for n in (
            "pre", "silu", "k_products", "k_squared", "sums", "rooted", "inverted", "k_done", "v_products", "v_done"))
        subs = lambda b: NSUB if b < NB else NSUB_P
        cache = io["cache_cmp_kv"].rearrange("n (q s) x g d -> (n q) (s x g d)", s=SUB)
        with nc.Block() as block:
            @block.gpsimd
            def _(pool):
                for b in range(NB):
                    if b >= 2:
                        pool.wait_ge(turned, 16 * (b - 1))
                    nc.gpsimd.indirect_dma_start(Z[:, b % 2, :], None, cache,
                                                 bass.IndirectOffsetOnAxis(K.idx[:, b:b + 1], 0)).then_inc(z_in[b % 2], 16)

            @block.sync
            def _(sp):
                sp.wait_ge(turned, 16 * (NB - 1))
                sp.dma_start(Z[0:NSUB_P, NB % 2, :],
                             io["cmp_kv_prompt"][0].rearrange("(n s) x g d -> n (s x g d)", s=SUB)).then_inc(zp_in, 16)

            @block.tensor
            def _(pe):
                pe.wait_ge(K.cmp_in, 16 * 10)
                nc.tensor.transpose(bank[6][:, 0:4 * SUB], per[:, :], G.ident[0:4 * SUB, 0:4 * SUB]).then_inc(setup, 1)
                pe.wait_ge(biased, 1)
                for x in range(2):
                    for js in range(2 * SUB):
                        last = nc.tensor.matmul(bank[7][:, x:x + 1], w1[:, x, js, :], pet[:, 2 * SUB * x + js:2 * SUB * x + js + 1],
                                                start=(js == 0), stop=(js == 2 * SUB - 1))
                last.then_inc(setup, 1)

                def second(u):
                    b, x = divmod(u, 2)
                    n = subs(b) - 1
                    pe.wait_ge(silu, u + 1)
                    if x == 0:
                        if b >= 1:
                            pe.wait_ge(v_ev, b)
                        else:
                            pe.wait_ge(biased, 2)
                        nc.tensor.matmul(bank[6][:, 0:2 * n].rearrange("p (g n) -> p g n", g=2), w2[:, 0, :],
                                         sl[:, 0, :, 0:n], start=True, stop=True).then_inc(k_mm, 1)
                    else:
                        pe.wait_ge(k_ev, b + 1)
                        for gp in range(2):
                            last = nc.tensor.matmul(bank[6][0:n, P * gp:P * gp + P], sl[:, 1, gp, 0:n], w2[:, 1, :],
                                                    start=True, stop=True)
                        last.then_inc(v_mm, 1)

                def square_sums(u):
                    b, x = divmod(u, 2)
                    n = subs(b) - 1
                    if x == 0:
                        pe.wait_ge(k_ev, b + 1)
                        if b >= 1:
                            pe.wait_ge(root, b)
                        nc.tensor.matmul(bank[7][:, 0:2 * n], G.blk[:, :], sq[:, 0:2 * n], start=True, stop=True).then_inc(ss, 1)

                def turn(u, i):
                    b, x = divmod(u, 2)
                    m, k = subs(b), 8 * u + i
                    if x == 0 and i == 0:
                        if b < NB:
                            pe.wait_ge(z_in[b % 2], 16 * (b // 2 + 1))
                        else:
                            pe.wait_ge(zp_in, 16)
                    if k >= 4:
                        pe.wait_ge(ev_a if k % 2 == 0 else ev_v, (k - 4) // 2 + 1)
                    for q in range(4):
                        col = 512 * (2 * i + q // 2) + 256 * x + P * (q % 2)
                        last = nc.tensor.transpose(bank[k % 4][:, P * q:P * q + m], Z[0:m, b % 2, col:col + P],
                                                   G.ident[0:m, 0:m])
                    last.then_inc(turned, 1)

                for i in range(8):
                    turn(0, i)
                for u in range(2 * NSEQ):
                    b, x = divmod(u, 2)
                    n = subs(b) - 1
                    pe.wait_ge(ev_a, 4 * u + 4)
                    pe.wait_ge(ev_v, 4 * u + 4)
                    if u >= 2:
                        pe.wait_ge(silu, u - 1)
                    o = bank[4 + x][:, 0:2 * n].rearrange("p (g n) -> p g n", g=2)
                    for js in range(2 * SUB):
                        if js % 4 == 0 and u + 1 < 2 * NSEQ:
                            turn(u + 1, js // 4)
                        if js == 8 and u:
                            second(u - 1)
                        if js == 28 and u:
                            square_sums(u - 1)
                        j, t = divmod(js, SUB)
                        last = nc.tensor.matmul(o, w1[:, x, js, :], XT[:, x, t, :, j:j + n],
                                                start=(js == 0), stop=(js == 2 * SUB - 1))
                    last.then_inc(pre, 1)
                second(2 * NSEQ - 1)

            def copy_rows(k, copy):
                u, i = divmod(k, 8)
                m = subs(u // 2)
                return copy(XT[:, u % 2, 2 * i:2 * i + 2, :, 0:m],
                            bank[k % 4][:, :].rearrange("p (s g n) -> p s g n", s=2, g=2)[:, :, :, 0:m])

            @block.scalar
            def _(act):
                act.wait_ge(setup, 1)
                nc.scalar.copy(pet[:, :], bank[6][:, 0:4 * SUB]).then_inc(biased, 1)
                act.wait_ge(setup, 2)
                nc.scalar.copy(bias[:, :], bank[7][:, 0:2]).then_inc(biased, 1)
                act.wait_ge(biased, 2)

                def second(u):
                    b, x = divmod(u, 2)
                    n = subs(b) - 1
                    if x == 0:
                        act.wait_ge(k_mm, b + 1)
                        if b >= 1:
                            act.wait_ge(kc, b)
                            act.wait_ge(ss, b)
                        nc.scalar.copy(kraw[:, 0:2 * n], bank[6][:, 0:2 * n])
                        nc.scalar.activation(sq[:, 0:2 * n], bank[6][:, 0:2 * n], ACT.Square).then_inc(k_ev, 1)
                    else:
                        act.wait_ge(v_mm, b + 1)
                        nc.scalar.copy(K.vc[0:n, b, :], bank[6][0:n, 0:2 * P]).then_inc(v_ev, 1)

                def roots(u):
                    b, x = divmod(u, 2)
                    n = subs(b) - 1
                    if x == 0:
                        act.wait_ge(ss, b + 1)
                        if b >= 1:
                            act.wait_ge(rt, b)
                        nc.scalar.activation(std[:, 0:2 * n], bank[7][:, 0:2 * n], ACT.Sqrt, scale=1.0 / HD,
                                             bias=G.eps[:, 0:1]).then_inc(root, 1)

                def rows(u, i):
                    if u < 2 * NSEQ:
                        act.wait_ge(turned, 8 * u + i + 1)
                        if u >= 2:
                            act.wait_ge(pre, u - 1)
                        copy_rows(8 * u + i, nc.scalar.copy).then_inc(ev_a, 1)

                for i in range(0, 8, 2):
                    rows(0, i)
                for u in range(2 * NSEQ):
                    rows(u + 1, 0)
                    rows(u + 1, 2)
                    if u:
                        second(u - 1)
                    rows(u + 1, 4)
                    rows(u + 1, 6)
                    if u:
                        roots(u - 1)
                    act.wait_ge(pre, u + 1)
                    b, x = divmod(u, 2)
                    n = subs(b) - 1
                    if u >= 2:
                        act.wait_ge(k_mm if x == 0 else v_mm, b)
                    nc.scalar.activation(sl[:, x, :, 0:n], bank[4 + x][:, 0:2 * n].rearrange("p (g n) -> p g n", g=2),
                                         ACT.Silu, bias=bias[:, x:x + 1]).then_inc(silu, 1)
                second(2 * NSEQ - 1)

            @block.vector
            def _(dve):
                nc.vector.memset(K.kc[:, NB, :, NCMP_P:NSUB_P], 0.0)

                def tail(u):
                    b, x = divmod(u, 2)
                    n = subs(b) - 1
                    if x == 0:
                        dve.wait_ge(root, b + 1)
                        if b >= 1:
                            dve.wait_ge(kc, b)
                        nc.vector.reciprocal(rstd[:, 0:2 * n], std[:, 0:2 * n]).then_inc(rt, 1)
                        dve.wait_ge(rt, b + 1)
                        g = lambda t: t[:, 0:2 * n].rearrange("p (g n) -> p g n", g=2)
                        nc.vector.scalar_tensor_tensor(out=K.kc[:, b, :, 0:n], in0=g(kraw), scalar=G.pv[:, C_KN:C_KN + 1],
                                                       in1=g(rstd), op0=ALU.mult, op1=ALU.mult).then_inc(kc, 1)

                def rows(u):
                    for i in range(1, 8, 2):
                        dve.wait_ge(turned, 8 * u + i + 1)
                        if u >= 2:
                            dve.wait_ge(pre, u - 1)
                        copy_rows(8 * u + i, nc.vector.tensor_copy).then_inc(ev_v, 1)

                rows(0)
                for u in range(2 * NSEQ):
                    if u + 1 < 2 * NSEQ:
                        rows(u + 1)
                    if u:
                        tail(u - 1)
                tail(2 * NSEQ - 1)


NBLK = PAST // HD + 1
TOP = 16
FORCED, TAKEN = 1e30, -1.0


def slot_chunk(gp, i):
    return 4 * gp + i


def stage_query(nc, G, K, Q, io):
    with Scope(nc, "qry") as s:
        xn = s.sb("xn", [P, DC, NT])
        w, wgt = s.sb("w_q", [P, DC, DC, P]), s.sb("w_gate", [P, DC, 48])
        sq, hs = s.sb("sq", [P, DC, NT]), s.sb("head_sums", [NH, 2, NT])
        sel = s.sb("gate_of", [48, 3, DC, P])
        bank = [s.bank(f"b{i}") for i in range(8)]
        w_in, g_in = [s.sem(f"w_in{i}") for i in range(2)], s.sem("gate_in")
        mm, ev, sqr, ss, root, inv, spread, normed = (s.sem(n) for n in (
            "products", "copied", "squared", "sums", "rooted", "inverted", "spread", "normed"))
        gmm, gev, zeroed = s.sem("gates_spread"), s.sem("gates_copied"), s.sem("zeroed")
        pstep, sel_ready = s.sem("pool_step"), s.sem("sel_ready")

        def ahead(sp):
            for k in range(DC):
                rows = io["w_qg"][0, P * k:P * k + P, :]
                for gp in range(2):
                    for g2 in range(2):
                        lo = 512 * gp + 256 * g2
                        sp.dma_start(w[:, k, 4 * gp:4 * gp + 4, HD * g2:HD * g2 + HD],
                                     rows[:, lo:lo + 256].rearrange("p (i d) -> p i d", d=HD)).then_inc(w_in[k // 4], 16)
            sp.dma_start(wgt[:, :, :], io["w_qg"][0, :, D:D + 48].rearrange("(k p) n -> p k n", p=P)).then_inc(g_in, 16)

        stage_norm(nc, G, "norm3", C_NG + 16, xn, ahead, sq, bank[0])
        with nc.Block() as block:
            @block.tensor
            def _(pe):
                for j in range(DC + 1):
                    if j == DC:
                        pe.wait_ge(g_in, 16)
                        pe.wait_ge(ev, 1)
                        pe.wait_ge(sqr, 1)
                    o = bank[j][:, 0:NT] if j < DC else bank[0][0:48, 0:NT]
                    for k in range(DC):
                        if j == 0 and k % 4 == 0:
                            pe.wait_ge(w_in[k // 4], 16 * 16)
                        last = nc.tensor.matmul(o, w[:, k, j, :] if j < DC else wgt[:, k, :], xn[:, k, :],
                                                start=(k == 0), stop=(k == DC - 1))
                    last.then_inc(mm, 1)
                pe.wait_ge(sqr, DC)
                for c in range(DC):
                    last = nc.tensor.matmul(bank[1][0:NH, 0:NT], G.head_of[:, c, :], sq[:, c, :], start=(c == 0), stop=(c == DC - 1))
                last.then_inc(ss, 1)
                pe.wait_ge(inv, 1)
                for c in range(DC):
                    if c < 2:
                        pe.wait_ge(ev, DC + 1)
                    nc.tensor.matmul(bank[c][:, 0:NT], G.to_head[:, c, :], hs[:, 1, :], start=True, stop=True).then_inc(spread, 1)
                pe.wait_ge(sel_ready, 1)
                pe.wait_ge(normed, DC)
                for br in range(3):
                    for c in range(DC):
                        last = nc.tensor.matmul(bank[br][:, NS * c:NS * c + NS], sel[:, br, c, :], Q.gates[:, NP:NT],
                                                start=True, stop=True)
                    last.then_inc(gmm, 1)
                for br in range(3):
                    for c in range(DC):
                        n = 8 * br + c
                        if n >= 5:
                            pe.wait_ge(gev, n - 1)
                        nc.tensor.matmul(bank[3 + n % 5][:, 0:NP], sel[:, br, c, :], Q.gates[:, 0:NP],
                                         start=True, stop=True).then_inc(gmm, 1)

            @block.scalar
            def _(act):
                for j in range(DC):
                    act.wait_ge(mm, j + 1)
                    nc.scalar.copy(Q.q[:, j, :], bank[j][:, 0:NT]).then_inc(ev, 1)
                    nc.scalar.activation(sq[:, j, :], bank[j][:, 0:NT], ACT.Square).then_inc(sqr, 1)
                act.wait_ge(mm, DC + 1)
                nc.scalar.activation(Q.gates[:, :], bank[0][0:48, 0:NT], ACT.Sigmoid).then_inc(ev, 1)
                act.wait_ge(ss, 1)
                nc.scalar.activation(hs[:, 0, :], bank[1][0:NH, 0:NT], ACT.Sqrt, scale=1.0 / HD,
                                     bias=G.eps[0:NH, 0:1]).then_inc(root, 1)
                for br in range(3):
                    act.wait_ge(gmm, br + 1)
                    nc.scalar.copy(Q.gs[:, br].rearrange("p c t -> p (c t)"), bank[br][:, 0:NS * DC]).then_inc(gev, 1)
                for n in range(3 * DC):
                    act.wait_ge(gmm, 4 + n)
                    nc.scalar.copy(Q.gp[:, n // 8, n % 8, :], bank[3 + n % 5][:, 0:NP]).then_inc(gev, 1)

            @block.gpsimd
            def _(pool):
                c = Chain(pool, pstep)
                c(nc.gpsimd.memset(sel[:, :, :, :], 0.0))
                for br in range(3):
                    for g2 in range(2):
                        part = sel[:, br, :, HD * g2:HD * g2 + HD].rearrange("r (gp i) d -> r gp i d", gp=2)
                        c(nc.gpsimd.affine_select(out=part, in_=part, compare_op=ALU.not_equal, fill=1.0, base=-16 * br - 4 * g2,
                                                  pattern=[[-8, 2], [-1, 4], [0, HD]], channel_multiplier=1))
                c(nc.gpsimd.affine_select(out=Q.covers[:, :], in_=G.ones[:, 0:NBLK], compare_op=ALU.is_gt, fill=0.0, base=HD,
                                          pattern=[[HD, NBLK]], channel_multiplier=-SUB))
                c(nc.gpsimd.affine_select(out=Q.covers[:, :], in_=Q.covers[:, :], compare_op=ALU.is_gt, fill=0.0, base=2 * SUB,
                                          pattern=[[-HD, NBLK]], channel_multiplier=SUB))
                pool.sem_inc(sel_ready, 1)

            @block.vector
            def _(dve):
                dve.wait_ge(root, 1)
                nc.vector.reciprocal(hs[:, 1, :], hs[:, 0, :]).then_inc(inv, 1)
                for c in range(DC):
                    dve.wait_ge(spread, c + 1)
                    nc.vector.scalar_tensor_tensor(out=Q.q[:, c, :], in0=Q.q[:, c, :], scalar=G.pv[:, C_KN + 3:C_KN + 4],
                                                   in1=bank[c][:, 0:NT], op0=ALU.mult, op1=ALU.mult).then_inc(normed, 1)
                dve.wait_ge(normed, DC)
                nc.vector.memset(Q.q2[:, :, :], 0.0).then_inc(zeroed, 1)
                dve.wait_ge(zeroed, 1)
                for b in range(NB):
                    for gp in range(2):
                        for g2 in range(2):
                            f, lo = slice(HD * g2, HD * g2 + HD), 32 * gp + 16 * g2
                            nc.vector.tensor_copy(Q.q2[f, 2 * b + gp, lo:lo + 16].rearrange("p (i t) -> p i t", t=DS),
                                                  Q.q[f, 4 * gp:4 * gp + 4, NP + DS * b:NP + DS * b + DS])


def stage_select(nc, G, K, Q, io):
    ROWS = 4 * 4 * DS
    with Scope(nc, "sel") as s:
        t4, tcol = s.sb("masks_by_t", [DS, 768]), s.sb("spread_t", [DS, ROWS])
        rep = s.sb("spread_rows", [P, NB, ROWS])
        p, st = s.sb("p", [ROWS, NB, NCMP]), s.sb("stats", [ROWS, 4, NB])
        pt, work, top = s.sb("p_t", [NCMP, 4, P]), s.sb("work", [P, NBLK]), s.sb("top", [P, 8])
        score, chosen = s.sb("score", [P, NBLK]), s.sb("chosen", [P, NBLK - 1])
        bank = [s.bank(f"b{i}") for i in range(8)]
        pstep, dstep, made, spread, sc, nm, ex = (s.sem(n) for n in (
            "pool_step", "dve_step", "made", "spread", "scores", "max_ready", "exps"))
        pn, turned, ptr, imp, cho, rows_mm, pv = (s.sem(n) for n in (
            "p_normed", "turned", "p_t_ready", "importance", "chosen", "mask_rows", "pv"))
        with nc.Block() as block:
            @block.gpsimd
            def _(pool):
                c = Chain(pool, pstep)
                sel = nc.gpsimd.affine_select
                c(nc.gpsimd.memset(t4[:, :], 0.0))
                c(nc.gpsimd.memset(tcol[:, :], 0.0))
                c(nc.gpsimd.memset(Q.mask_a[:, :], 0.0))
                c(nc.gpsimd.memset(Q.mask_b[:, :], 0.0))
                v = tcol[:, :].rearrange("p (x t) -> p x t", t=DS)
                c(sel(out=v, in_=v, compare_op=ALU.not_equal, fill=1.0, base=0, pattern=[[0, 16], [-1, DS]], channel_multiplier=1))
                v = t4[:, 0:512].rearrange("p (w n) -> p w n", w=4)
                c(sel(out=v, in_=v, compare_op=ALU.is_gt, fill=NEG, base=0, pattern=[[1, 4], [4, P]], channel_multiplier=-1))
                v = t4[:, 512:768].rearrange("p (b c t) -> p b c t", b=NB, c=NB)
                c(sel(out=v, in_=v, compare_op=ALU.is_equal, fill=NEG, base=0, pattern=[[1, NB], [-1, NB], [0, DS]], channel_multiplier=0))
                c(sel(out=v, in_=v, compare_op=ALU.is_ge, fill=NEG, base=0, pattern=[[0, NB], [0, NB], [-1, DS]], channel_multiplier=1))
                v = Q.mask_a[:, :].rearrange("p (x k) -> p x k", x=2)
                c(sel(out=v, in_=v, compare_op=ALU.is_ge, fill=NEG, base=P, pattern=[[0, 2], [-1, NP]], channel_multiplier=1))
                v = Q.mask_b[:, 0:2 * P].rearrange("p (x k) -> p x k", x=2)
                c(sel(out=v, in_=v, compare_op=ALU.is_ge, fill=NEG, base=0, pattern=[[0, 2], [-1, P]], channel_multiplier=1))
                v = Q.mask_b[:, 2 * P:2 * P + 32].rearrange("p (x n) -> p x n", x=2)
                c(sel(out=v, in_=v, compare_op=ALU.is_ge, fill=NEG, base=1 - 2 * SUB, pattern=[[P, 2], [-SUB, SUB]], channel_multiplier=1))
                pool.sem_inc(made, 1)

            @block.tensor
            def _(pe):
                for b in range(NB):
                    for gp in range(2):
                        last = nc.tensor.matmul(bank[b // 4][0:ROWS, P * (b % 4):P * (b % 4) + NCMP], Q.q2[:, 2 * b + gp, :],
                                                K.kc[:, b, gp, 0:NCMP], start=(gp == 0), stop=(gp == 1))
                last.then_inc(sc, 1)
                pe.wait_ge(made, 1)
                nc.tensor.matmul(bank[2][0:ROWS, :], tcol[:, :], t4[:, 0:512], start=True, stop=True)
                nc.tensor.matmul(bank[3][0:ROWS, 0:256], tcol[:, :], t4[:, 512:768], start=True, stop=True).then_inc(spread, 1)
                pe.wait_ge(pn, 1)
                for b in range(NB):
                    last = nc.tensor.transpose(bank[4][0:NCMP, ROWS * b:ROWS * b + ROWS], p[:, b, :], G.ident[0:ROWS, 0:ROWS])
                last.then_inc(turned, 1)
                pe.wait_ge(ptr, 1)
                for i in range(4):
                    last = nc.tensor.matmul(bank[5][:, 0:NBLK], pt[:, i, :], Q.covers[0:NCMP, :], start=(i == 0), stop=(i == 3))
                last.then_inc(imp, 1)
                pcols = pt[:, :, :].rearrange("n i (b g t) -> n b g i t", b=NB, g=4)
                for b in range(NB):
                    for gp in range(2):
                        o = bank[6][:, 64 * b + 32 * gp:64 * b + 32 * gp + 32].rearrange("p (g i t) -> p g i t", g=2, i=4)
                        last = nc.tensor.matmul(o, K.vc[0:NCMP, b, P * gp:P * gp + P], pcols[:, b, 2 * gp:2 * gp + 2],
                                                start=True, stop=True)
                last.then_inc(pv, 1)
                pe.wait_ge(cho, 1)
                for b in range(NB):
                    last = nc.tensor.matmul(bank[7][0:ROWS, 32 * b:32 * b + 32], rep[:, b, :], chosen[:, :], start=True, stop=True)
                last.then_inc(rows_mm, 1)

            @block.scalar
            def _(act):
                act.wait_ge(nm, 1)
                for b in range(NB):
                    last = nc.scalar.activation(p[:, b, :], bank[b // 4][0:ROWS, P * (b % 4):P * (b % 4) + NCMP], ACT.Exp,
                                                scale=SCALE, bias=st[:, 1, b:b + 1], accum_out=st[:, 2, b:b + 1])
                last.then_inc(ex, 1)
                act.wait_ge(turned, 1)
                nc.scalar.copy(pt[:, :, :].rearrange("n i (x t) -> n x i t", t=DS),
                               bank[4][0:NCMP, :].rearrange("n (x i t) -> n x i t", i=4, t=DS)).then_inc(ptr, 1)

            @block.vector
            def _(dve):
                step = Chain(dve, dstep)
                for b in range(NB):
                    cols = G.ident[:, 16 * b:16 * b + 16].rearrange("p (g t) -> p g t", t=DS)
                    nc.vector.tensor_copy(rep[:, b, :].rearrange("p (g i t) -> p g i t", g=4, i=4),
                                          cols.unsqueeze(2).to_broadcast([P, 4, 4, DS]))
                dve.wait_ge(sc, 1)
                for half in range(2):
                    last = nc.vector.reduce_max(st[:, 0, 4 * half:4 * half + 4],
                                                bank[half][0:ROWS, :].rearrange("p (b n) -> p b n", n=P)[:, :, 0:NCMP], axis=AX)
                step(last)
                nc.vector.tensor_scalar(st[:, 1, :], st[:, 0, :], -SCALE, None, ALU.mult).then_inc(nm, 1)
                dve.wait_ge(spread, 1)
                nc.vector.tensor_copy(Q.mask_win[:, :], bank[2][0:ROWS, :])
                nc.vector.tensor_copy(Q.mask_new[:, :, :], bank[3][0:ROWS, 0:256].rearrange("p (b c) -> p b c", b=NB))
                dve.wait_ge(ex, 1)
                step(nc.vector.reciprocal(st[:, 3, :], st[:, 2, :]))
                nc.vector.tensor_tensor(p[:, :, :], p[:, :, :], st[:, 3, :].unsqueeze(2).to_broadcast([ROWS, NB, NCMP]),
                                        ALU.mult).then_inc(pn, 1)
                dve.wait_ge(imp, 1)
                step(nc.vector.tensor_copy(score[:, :], bank[5][:, 0:NBLK]))
                step(nc.vector.memset(score[:, 0:1], FORCED))
                step(nc.vector.memset(score[:, NBLK - 2:NBLK], FORCED))
                src = score
                for r in range(TOP // 8):
                    step(nc.vector.max(top[:, :], src[:, :]))
                    step(nc.vector.match_replace(work[:, :], top[:, :], src[:, :], TAKEN))
                    src = work
                step(nc.vector.tensor_scalar(chosen[:, :], work[:, 0:NBLK - 1], TAKEN, None, ALU.is_equal))
                nc.vector.tensor_scalar(chosen[:, :], chosen[:, :], -1.0, -NEG, ALU.add, ALU.mult).then_inc(cho, 1)
                dve.wait_ge(pv, 1)
                for gp in range(2):
                    for g2 in range(2):
                        f = slice(HD * g2, HD * g2 + HD)
                        src = bank[6][f, :].rearrange("p (b x i t) -> p x i b t", b=NB, x=4, i=4)[:, 2 * gp + g2]
                        for i in range(4):
                            nc.vector.tensor_tensor(Q.o[f, 4 * gp + i, NP:NT].rearrange("p (b t) -> p b t", t=DS), src[:, i],
                                                    Q.gs[f, 0, 4 * gp + i, :].rearrange("p (b t) -> p b t", t=DS), ALU.mult)
                dve.wait_ge(rows_mm, 1)
                nc.vector.tensor_copy(Q.mask_slc[:, :, :], bank[7][0:ROWS, 0:256].rearrange("p (b c) -> p b c", b=NB))


def stage_sample(nc, G, K, Q, io):
    ROWS, WR = 4 * 4 * DS, 4
    with Scope(nc, "smp") as s:
        NZ = 3
        third = s.sb("rows_c", [P, RW])
        Z = [K.Z[:, 0], K.Z[:, 1], third[:, :]]
        WK, WV = (s.sb(n, [P, 2, WR, 2 * P]) for n in ("win_key_rows", "win_value_rows"))
        KT, KW = s.sb("keys_t", [P, 2, PAST]), s.sb("win_keys_t", [P, 2, WR * P])
        p = s.sb("p", [ROWS, PAST + 512 + 64])
        pt = s.sb("p_t", [P, 3, 8, ROWS])
        st, tmp = s.sb("stats", [ROWS, 8]), s.sb("gated", [P, 2, 2, 16])
        inv, o_rows = s.sb("inverse_sums", [ROWS, 2]), s.sb("o_rows", [ROWS, 2, 2 * P])
        bank = [s.bank(f"b{i}") for i in range(8)]
        z_in = K.z_in
        wk_in, wv_in = ([s.sem(f"{n}_in{i}") for i in range(2)] for n in ("win_keys", "win_values"))
        turned, kev, sc, nm, ex, pn = (s.sem(n) for n in (
            "turned", "keys_copied", "scores", "max_ready", "exps", "inverse_ready"))
        oturned = s.sem("o_turned")
        pmm, pev, pv, oread, oev, dstep = (s.sem(n) for n in ("p_turned", "p_copied", "pv", "o_read", "o_done", "dve_step"))
        cache = io["cache_slc_kv"].rearrange("n (q s) x g d -> (n q) (s x g d)", s=SUB)
        NTB = SUB * 2 // 4 + WR * 2 // 4
        NPT = 3
        o_win, o_new = PAST, PAST + 512
        ring = lambda k: bank[6 + k % 2]
        with nc.Block() as block:
            @block.gpsimd
            def _(pool):
                for b in range(2, NB):
                    if b >= NZ:
                        pool.wait_ge(pv, b - NZ + 1)
                    nc.gpsimd.indirect_dma_start(Z[b % NZ], None, cache,
                                                 bass.IndirectOffsetOnAxis(K.idx[:, b:b + 1], 0)).then_inc(z_in[b % NZ], 16)

            @block.sync
            def _(sp):
                state = lambda b, x: io["state_win_kv"][b].rearrange("(n w) x g d -> n w x (g d)", w=WR)[:, :, x, :]
                for b in range(NB):
                    if b >= 2:
                        sp.wait_ge(turned, NTB * (b - 1))
                    sp.dma_start(WK[:, b % 2], state(b, 0)).then_inc(wk_in[b % 2], 16)
                    if b >= 2:
                        sp.wait_ge(pv, b - 1)
                    sp.dma_start(WV[:, b % 2], state(b, 1)).then_inc(wv_in[b % 2], 16)

            @block.tensor
            def _(pe):
                def turn_keys(b):
                    for k in range(NTB):
                        if k == 0:
                            pe.wait_ge(z_in[b % NZ], 16 * (b // NZ + 1))
                        if k == 8:
                            pe.wait_ge(wk_in[b % 2], 16 * (b // 2 + 1))
                        if k >= 2:
                            pe.wait_ge(kev, NTB * b + k - 1)
                        elif b >= 2:
                            pe.wait_ge(pev, NPT * (b - 2) + k + 2)
                        for q in range(4):
                            r, gp = (4 * (k % 8) + q) // 2, q % 2
                            src = Z[b % NZ][:, 512 * r + P * gp:512 * r + P * gp + P] if k < 8 else WK[:, b % 2, r, P * gp:P * gp + P]
                            last = nc.tensor.transpose(ring(k)[:, P * q:P * q + P], src, G.ident[:, :])
                        last.then_inc(turned, 1)

                def scores(b):
                    pe.wait_ge(kev, NTB * (b + 1))
                    if b:
                        pe.wait_ge(nm, b)
                    for gp in range(2):
                        q = Q.q2[:, 2 * b + gp, :]
                        f = dict(start=(gp == 0), stop=(gp == 1))
                        for k in range(4):
                            nc.tensor.matmul(bank[k][0:ROWS, :], q, KT[:, gp, 512 * k:512 * k + 512], **f)
                        nc.tensor.matmul(bank[4][0:ROWS, :], q, KW[:, gp, :], **f)
                    if b >= 2:
                        pe.wait_ge(oev, b - 1)
                    for br in range(2):
                        for gp in range(2):
                            last = nc.tensor.matmul(bank[5][0:ROWS, NS * br:NS * br + NS], Q.q2[:, 2 * b + gp, :],
                                                    K.kt[:, 2 * br + gp, NP:NT], start=(gp == 0), stop=(gp == 1))
                    last.then_inc(sc, 1)

                def turn_p(b):
                    pe.wait_ge(ex, b + 1)
                    for n in range(NPT):
                        if n == 0 or (n == 1 and not b):
                            pe.wait_ge(kev, NTB * min(b + 2, NB))
                        elif n == 1:
                            pe.wait_ge(oread, b)
                        else:
                            pe.wait_ge(pev, NPT * b + 1)
                        for j in range(8 * n, min(8 * n + 8, 22)):
                            if j < 20:
                                src, m = p[:, P * j:P * j + P], P
                            else:
                                src, m = p[:, o_new + NS * (j - 20):o_new + NS * (j - 20) + NS], NS
                            last = nc.tensor.transpose(ring(NTB + 1 + n)[0:m, ROWS * (j % 8):ROWS * (j % 8) + ROWS], src,
                                                       G.ident[0:ROWS, 0:ROWS])
                        last.then_inc(pmm, 1)

                def values(b):
                    pe.wait_ge(pev, NPT * (b + 1))
                    pe.wait_ge(wv_in[b % 2], 16 * (b // 2 + 1))
                    pe.wait_ge(kev, NTB * min(b + 3, NB))
                    for br in range(2):
                        js = list(range(16)) + [20] if br == 0 else list(range(16, 20)) + [21]
                        for j in js:
                            if j < 16:
                                v = Z[b % NZ][:, 512 * j + 256:512 * j + 512]
                            elif j < 20:
                                v = WV[:, b % 2, j - 16, :]
                            else:
                                v = K.vn[0:NS, 2, br, :]
                            m = P if j < 20 else NS
                            last = nc.tensor.matmul(ring(NTB)[0:ROWS, 2 * P * br:2 * P * br + 2 * P], pt[0:m, j // 8, j % 8, :], v,
                                                    start=(j == js[0]), stop=(j == js[-1]))
                    last.then_inc(pv, 1)

                def turn_out(b):
                    pe.wait_ge(oread, b + 1)
                    for x in range(4):
                        last = nc.tensor.transpose(bank[5][:, P + ROWS * x:P + ROWS * x + ROWS],
                                                   o_rows[:, x // 2, P * (x % 2):P * (x % 2) + P], G.ident[0:ROWS, 0:ROWS])
                    last.then_inc(oturned, 1)

                turn_keys(0)
                scores(0)
                for b in range(NB):
                    if b + 1 < NB:
                        turn_keys(b + 1)
                    if b:
                        values(b - 1)
                    turn_p(b)
                    if b:
                        turn_out(b - 1)
                    if b + 1 < NB:
                        scores(b + 1)
                values(NB - 1)
                turn_out(NB - 1)

            @block.scalar
            def _(act):
                def keys(b):
                    for k in range(NTB):
                        act.wait_ge(turned, NTB * b + k + 1)
                        if b:
                            act.wait_ge(sc, b)
                        dst, r = (KT, 2 * k) if k < 8 else (KW, 2 * (k - 8))
                        nc.scalar.copy(dst[:, :, P * r:P * r + 2 * P].rearrange("p g (r n) -> p g r n", r=2),
                                       ring(k)[:, :].rearrange("p (r g n) -> p g r n", r=2, g=2)).then_inc(kev, 1)

                keys(0)
                for b in range(NB):
                    if b + 1 < NB:
                        keys(b + 1)
                    act.wait_ge(nm, b + 1)
                    nc.scalar.activation(p[:, 0:PAST], p[:, 0:PAST], ACT.Exp, scale=SCALE, bias=st[:, 2:3], accum_out=st[:, 4:5])
                    nc.scalar.activation(p[:, o_new:o_new + NS], p[:, o_new:o_new + NS], ACT.Exp, scale=SCALE,
                                         bias=st[:, 2:3], accum_out=st[:, 5:6])
                    nc.scalar.activation(p[:, o_win:o_new], p[:, o_win:o_new], ACT.Exp, scale=SCALE, bias=st[:, 3:4],
                                         accum_out=st[:, 6:7])
                    nc.scalar.activation(p[:, o_new + NS:], p[:, o_new + NS:], ACT.Exp, scale=SCALE, bias=st[:, 3:4],
                                         accum_out=st[:, 7:8]).then_inc(ex, 1)
                    for n in range(NPT):
                        act.wait_ge(pmm, NPT * b + n + 1)
                        if b:
                            act.wait_ge(pv, b)
                        src = ring(NTB + 1 + n)
                        if n < 2:
                            last = nc.scalar.copy(pt[:, n].rearrange("p k r -> p (k r)"), src[:, :])
                        else:
                            nc.scalar.copy(pt[:, 2, 0:4].rearrange("p k r -> p (k r)"), src[:, 0:4 * ROWS])
                            last = nc.scalar.copy(pt[0:NS, 2, 4:6].rearrange("p k r -> p (k r)"), src[0:NS, 4 * ROWS:6 * ROWS])
                        last.then_inc(pev, 1)

            @block.vector
            def _(dve):
                step = Chain(dve, dstep)
                halves = lambda t: t.rearrange("p (x c) -> p x c", x=2)

                def mask(b):
                    dve.wait_ge(sc, b + 1)
                    if b:
                        dve.wait_ge(pmm, NPT * b)
                    for k in range(4):
                        m = Q.mask_slc[:, b, :].unsqueeze(1).unsqueeze(3).to_broadcast([ROWS, 4, 32, 4])
                        nc.vector.tensor_tensor(p[:, 512 * k:512 * k + 512].rearrange("p (s c n) -> p s c n", s=4, n=4),
                                                bank[k][0:ROWS, :].rearrange("p (s c n) -> p s c n", s=4, n=4), m, ALU.add)
                    nc.vector.tensor_tensor(p[:, o_win:o_new], bank[4][0:ROWS, :], Q.mask_win[:, :], ALU.add)
                    step(nc.vector.tensor_tensor(halves(p[:, o_new:]), halves(bank[5][0:ROWS, 0:2 * NS]),
                                                 Q.mask_new[:, b, :].unsqueeze(1).to_broadcast([ROWS, 2, NS]), ALU.add))
                    nc.vector.reduce_max(st[:, 0:1], p[:, 0:PAST], axis=AX)
                    nc.vector.reduce_max(st[:, 1:2], p[:, o_win:o_new], axis=AX)
                    step(nc.vector.reduce_max(st[:, 4:6], halves(p[:, o_new:]), axis=AX))
                    step(nc.vector.tensor_tensor(st[:, 2:4], st[:, 0:2], st[:, 4:6], ALU.max))
                    nc.vector.tensor_scalar(st[:, 2:4], st[:, 2:4], -SCALE, None, ALU.mult).then_inc(nm, 1)

                def outputs(b):
                    dve.wait_ge(pv, b + 1)
                    for br in range(2):
                        last = nc.vector.tensor_scalar(o_rows[:, br, :], ring(NTB)[0:ROWS, 2 * P * br:2 * P * br + 2 * P],
                                                       inv[:, br:br + 1], None, ALU.mult)
                    last.then_inc(oread, 1)
                    dve.wait_ge(oturned, b + 1)
                    ts = slice(NP + DS * b, NP + DS * b + DS)
                    for br in range(2):
                        for gp in range(2):
                            for g2 in range(2):
                                f, cs = slice(HD * g2, HD * g2 + HD), slice(4 * gp, 4 * gp + 4)
                                col = P + ROWS * (2 * br + gp) + 32 * gp + 16 * g2
                                last = nc.vector.tensor_tensor(tmp[f, br, gp, :].rearrange("p (i t) -> p i t", t=DS),
                                                               bank[5][f, col:col + 16].rearrange("p (i t) -> p i t", t=DS),
                                                               Q.gs[f, 1 + br, cs, DS * b:DS * b + DS], ALU.mult)
                    step(last)
                    step(nc.vector.tensor_tensor(tmp[:, 0], tmp[:, 0], tmp[:, 1], ALU.add))
                    nc.vector.tensor_tensor(Q.o[:, :, ts], Q.o[:, :, ts],
                                            tmp[:, 0].rearrange("p g (i t) -> p (g i) t", t=DS), ALU.add).then_inc(oev, 1)
                    dve.wait_ge(oev, b + 1)

                mask(0)
                for b in range(NB):
                    if b:
                        outputs(b - 1)
                    dve.wait_ge(ex, b + 1)
                    step(nc.vector.tensor_tensor(st[:, 0:2], st[:, 4:8:2], st[:, 5:8:2], ALU.add))
                    nc.vector.reciprocal(inv[:, :], st[:, 0:2]).then_inc(pn, 1)
                    dve.wait_ge(pn, b + 1)
                    if b + 1 < NB:
                        mask(b + 1)
                outputs(NB - 1)


def stage_prompt(nc, G, K, Q, io):
    assert NP // HD <= TOP and NP <= 512
    with Scope(nc, "prm") as s:
        A, B = s.sb("p_late", [P, 2, 512]), s.sb("p_early", [P, 2, 288])
        st = s.sb("stats", [P, 2, 4, 6])
        pt, ptc = s.sb("p_t", [P, 2, 6, P]), s.sb("p_cmp_t", [NSUB_P, 2, 2 * P])
        tmp = s.sb("gated", [P, 3, NP])
        bank = [s.bank(f"b{i}") for i in range(8)]
        sc, nm, ex, pn, pmm, pev, pv, oev, dstep = (s.sem(n) for n in (
            "scores", "max_ready", "exps", "p_normed", "p_turned", "p_copied", "pv", "o_done", "dve_step"))
        cache = io["cache_slc_kv"].rearrange("n (q s) x g d -> (n q) (s x g d)", s=SUB)
        with nc.Block() as block:
            @block.gpsimd
            def _(pool):
                for b in range(2):
                    nc.gpsimd.indirect_dma_start(K.Z[:, b], None, cache,
                                                 bass.IndirectOffsetOnAxis(K.idx[:, b:b + 1], 0)).then_inc(K.z_in[b], 16)

            @block.tensor
            def _(pe):
                def scores(h):
                    c, g2 = divmod(h, 2)
                    gp, f = c // 4, slice(HD * g2, HD * g2 + HD)
                    if h >= 2:
                        pe.wait_ge(nm, h - 1)
                    a, b = bank[2 * g2], bank[2 * g2 + 1]
                    q0, q1 = Q.q[f, c, 0:P], Q.q[f, c, P:NP]
                    for br in range(2):
                        nc.tensor.matmul(a[:, 256 * br:256 * br + 256], q1, K.kt[f, 2 * br + gp, 0:NP], start=True, stop=True)
                        nc.tensor.matmul(b[:, P * br:P * br + P], q0, K.kt[f, 2 * br + gp, 0:P], start=True, stop=True)
                    for x, q in enumerate((q0, q1)):
                        last = nc.tensor.matmul(b[:, 256 + 16 * x:272 + 16 * x], q, K.kc[f, NB, gp, 0:NSUB_P], start=True, stop=True)
                    last.then_inc(sc, 1)

                def turn(h):
                    g2 = h % 2
                    pe.wait_ge(pn, h + 1)
                    if h:
                        pe.wait_ge(pev, h)
                    for k in range(4):
                        nc.tensor.transpose(bank[4][:, P * k:P * k + P], A[:, g2, P * k:P * k + P], G.ident[:, :])
                    for k in range(2):
                        nc.tensor.transpose(bank[5][:, P * k:P * k + P], B[:, g2, P * k:P * k + P], G.ident[:, :])
                    for x in range(2):
                        last = nc.tensor.transpose(bank[5][0:NSUB_P, 256 + P * x:384 + P * x],
                                                   B[:, g2, 256 + 16 * x:272 + 16 * x], G.ident[:, :])
                    last.then_inc(pmm, 1)

                def values(h):
                    pe.wait_ge(pev, h + 1)
                    if h:
                        pe.wait_ge(oev, h)
                    gp = h // 8
                    col, o = slice(P * gp, P * gp + P), bank[6]
                    for br in range(2):
                        nc.tensor.matmul(o[:, 256 * br:256 * br + P], K.vn[:, 0, br, col], pt[:, h % 2, 4 + br, :], start=True, stop=True)
                        for k in range(2):
                            nc.tensor.matmul(o[:, 256 * br + P:256 * br + 256], K.vn[:, k, br, col], pt[:, h % 2, 2 * br + k, :],
                                             start=(k == 0), stop=(k == 1))
                    nc.tensor.matmul(bank[7][:, 0:NP], K.vc[0:NCMP_P, NB, col], ptc[0:NCMP_P, h % 2, :], start=True, stop=True).then_inc(pv, 1)

                scores(0)
                scores(1)
                for h in range(NH):
                    turn(h)
                    if h + 2 < NH:
                        scores(h + 2)
                    values(h)

            @block.scalar
            def _(act):
                def copies(h):
                    act.wait_ge(pmm, h + 1)
                    if h >= 2:
                        act.wait_ge(pv, h - 1)
                    nc.scalar.copy(pt[:, h % 2, 0:4].rearrange("p k q -> p (k q)"), bank[4][:, :])
                    nc.scalar.copy(pt[:, h % 2, 4:6].rearrange("p k q -> p (k q)"), bank[5][:, 0:256])
                    nc.scalar.copy(ptc[:, h % 2, :], bank[5][0:NSUB_P, 256:512]).then_inc(pev, 1)

                def exps(h):
                    g2 = h % 2
                    act.wait_ge(nm, h + 1)
                    parts = [(A[:, g2, 0:256], 0), (A[:, g2, 256:512], 1), (B[:, g2, 0:P], 2), (B[:, g2, P:256], 3),
                             (B[:, g2, 256:272], 4), (B[:, g2, 272:288], 5)]
                    for ap, k in parts:
                        last = nc.scalar.activation(ap, ap, ACT.Exp, scale=SCALE, bias=st[:, g2, 1, k:k + 1],
                                                    accum_out=st[:, g2, 2, k:k + 1])
                    last.then_inc(ex, 1)

                exps(0)
                for h in range(NH):
                    if h + 1 < NH:
                        exps(h + 1)
                    copies(h)

            @block.vector
            def _(dve):
                step = Chain(dve, dstep)
                v = lambda t: t.rearrange("p (x k) -> p x k", x=2)

                def mask(h):
                    g2 = h % 2
                    dve.wait_ge(sc, h + 1)
                    if h >= 2:
                        dve.wait_ge(pmm, h - 1)
                    nc.vector.tensor_tensor(A[:, g2, :], bank[2 * g2][:, :], Q.mask_a[:, :], ALU.add)
                    step(nc.vector.tensor_tensor(B[:, g2, :], bank[2 * g2 + 1][:, 0:288], Q.mask_b[:, :], ALU.add))
                    nc.vector.reduce_max(st[:, g2, 0, 0:2], v(A[:, g2, :]), axis=AX)
                    nc.vector.reduce_max(st[:, g2, 0, 2:4], v(B[:, g2, 0:256]), axis=AX)
                    step(nc.vector.reduce_max(st[:, g2, 0, 4:6], v(B[:, g2, 256:288]), axis=AX))
                    nc.vector.tensor_scalar(st[:, g2, 1, :], st[:, g2, 0, :], NEG / 1e10, -SCALE, ALU.max, ALU.mult).then_inc(nm, 1)

                def norm(h):
                    g2 = h % 2
                    dve.wait_ge(ex, h + 1)
                    step(nc.vector.tensor_scalar(st[:, g2, 3, :], st[:, g2, 2, :], 1e-30, None, ALU.max))
                    step(nc.vector.reciprocal(st[:, g2, 0, :], st[:, g2, 3, :]))
                    r = lambda a, b, n: st[:, g2, 0, a:b].unsqueeze(2).to_broadcast([P, 2, n])
                    nc.vector.tensor_tensor(v(A[:, g2, :]), v(A[:, g2, :]), r(0, 2, 256), ALU.mult)
                    nc.vector.tensor_tensor(v(B[:, g2, 0:256]), v(B[:, g2, 0:256]), r(2, 4, P), ALU.mult)
                    nc.vector.tensor_tensor(v(B[:, g2, 256:288]), v(B[:, g2, 256:288]), r(4, 6, 16), ALU.mult).then_inc(pn, 1)

                def outputs(h):
                    c, f = h // 2, slice(HD * (h % 2), HD * (h % 2) + HD)
                    dve.wait_ge(pv, h + 1)
                    nc.vector.tensor_tensor(tmp[f, 0, :], bank[7][f, 0:NP], Q.gp[f, 0, c, :], ALU.mult)
                    for br in range(2):
                        last = nc.vector.tensor_tensor(tmp[f, 1 + br, :], bank[6][f, 256 * br:256 * br + 256],
                                                       Q.gp[f, 1 + br, c, :], ALU.mult)
                    last.then_inc(oev, 1)
                    dve.wait_ge(oev, h + 1)
                    step(nc.vector.tensor_tensor(tmp[f, 0, :], tmp[f, 0, :], tmp[f, 1, :], ALU.add))
                    step(nc.vector.tensor_tensor(Q.o[f, c, 0:NP], tmp[f, 0, :], tmp[f, 2, :], ALU.add))

                mask(0)
                for h in range(NH):
                    if h + 1 < NH:
                        mask(h + 1)
                    norm(h)
                    if h:
                        outputs(h - 1)
                outputs(NH - 1)


def stage_attn_out(nc, G, Q, io):
    with Scope(nc, "aout") as s:
        wo = s.sb("wo", [P, DC, D])
        bank = [s.bank(f"b{i}") for i in range(8)]
        w_in, mm, ev = [s.sem(f"w_in{i}") for i in range(2)], s.sem("products"), s.sem("added")
        with nc.Block() as block:
            @block.sync
            def _(sp):
                for gp in range(2):
                    for g2 in range(2):
                        lo = 512 * gp + 256 * g2
                        sp.dma_start(wo[HD * g2:HD * g2 + HD, 4 * gp:4 * gp + 4, :],
                                     io["w_o"][0, lo:lo + 256, :].rearrange("(i d) n -> d i n", d=HD)).then_inc(w_in[gp], 16)

            @block.tensor
            def _(pe):
                for gp in range(2):
                    pe.wait_ge(w_in[gp], 32)
                    for c in range(DC):
                        for k in range(4 * gp, 4 * gp + 4):
                            last = nc.tensor.matmul(bank[c][:, 0:NT], wo[:, k, P * c:P * c + P], Q.o[:, k, :],
                                                    start=(k == 0), stop=(k == DC - 1))
                        if gp == 1:
                            last.then_inc(mm, 1)

            @block.vector
            def _(dve):
                for c in range(DC):
                    dve.wait_ge(mm, c + 1)
                    nc.vector.tensor_tensor(G.h[:, c, :], G.h[:, c, :], bank[c][:, 0:NT], ALU.add).then_inc(ev, 1)


TAU = -(-NT // P)
TILES = ((0, P), (1, P), (2, NS))


def stage_route(nc, G, M, io):
    with Scope(nc, "route") as s:
        xn = s.sb("xn", [P, DC, NT])
        wr, lo, ex = s.sb("w_router", [P, DC, NE]), s.sb("logits", [P, 3, NE]), s.sb("exps", [P, 3, NE])
        above, tie, first = s.sb("above", [P, 3, NE, NE]), s.sb("tie", [P, 3, NE, NE]), s.sb("first", [P, NE, NE])
        rank, top, den = s.sb("rank", [P, 3, NE]), s.sb("top", [P, 3]), s.sb("sum", [P, 3])
        pick, pos, num = s.sb("pick", [P, 3, NE]), s.sb("pos", [P, 3, NE]), s.sb("slot_numbers", [P, P], I32)
        before = s.sb("before", [P, P])
        some = s.sb("some_more", [1, 1])
        more, acc = s.sb("more_blocks", [1, 2 * NE]), s.sb("blocks_so_far", [1, 2, 2 * NE])
        bank = [s.bank(f"b{i}") for i in range(8)]
        w_in, made, mm, step_s, less, exd, picked, placed, turned, ev = (s.sem(n) for n in (
            "w_in", "made", "products", "dve_step", "less_max", "exps", "picked", "placed", "turned", "copied"))
        stage_norm(nc, G, "norm4", C_NG + 24, xn, lambda sp: sp.dma_start(
            wr[:, :, :], io["moe_router"][0].rearrange("(k p) n -> p k n", p=P)).then_inc(w_in, 16),
                   s.sb("norm_work", [P, 2, NT]), bank[0])
        with nc.Block() as block:
            @block.gpsimd
            def _(pool):
                nc.gpsimd.affine_select(out=first[:, :, :], in_=G.ones[:, 0:NE * NE].rearrange("p (j i) -> p j i", i=NE),
                                        compare_op=ALU.is_gt, fill=0.0, base=0, pattern=[[1, NE], [-1, NE]],
                                        channel_multiplier=0).then_inc(made, 1)
                nc.gpsimd.affine_select(out=before[:, :], in_=G.ones[:, :], compare_op=ALU.is_gt, fill=0.0, base=0,
                                        pattern=[[1, P]], channel_multiplier=-1).then_inc(made, 1)
                nc.gpsimd.iota(num[:, :], pattern=[[1, P]], base=0, channel_multiplier=0).then_inc(made, 1)

            @block.tensor
            def _(pe):
                pe.wait_ge(w_in, 16)
                for t, m in TILES:
                    for k in range(DC):
                        last = nc.tensor.matmul(bank[0][0:m, NE * t:NE * t + NE], xn[:, k, P * t:P * t + m], wr[:, k, :],
                                                start=(k == 0), stop=(k == DC - 1))
                last.then_inc(mm, 1)
                for n in range(6):
                    t, m = TILES[n // 2]
                    for c in range(4):
                        last = nc.tensor.transpose(bank[2 + n][0:m, P * c:P * c + P], xn[:, 4 * (n % 2) + c, P * t:P * t + m],
                                                   G.ident[:, :])
                    last.then_inc(turned, 1)
                pe.wait_ge(picked, 1)
                pe.wait_ge(made, 3)
                for t, m in TILES:
                    for i in range(t + 1):
                        k = TILES[i][1]
                        nc.tensor.matmul(bank[1][0:m, NE * t:NE * t + NE], (before if i == t else G.ones)[0:k, 0:m],
                                         pick[0:k, i, :], start=(i == 0), stop=(i == t))
                for t, m in TILES:
                    last = nc.tensor.matmul(bank[1][:, 3 * NE:4 * NE], G.ones[0:m, :], pick[0:m, t, :],
                                            start=(t == 0), stop=(t == 2))
                last.then_inc(placed, 1)

            @block.scalar
            def _(act):
                for n in range(6):
                    t, m = TILES[n // 2]
                    act.wait_ge(turned, n + 1)
                    nc.scalar.copy(M.xt[0:m, t, 512 * (n % 2):512 * (n % 2) + 512], bank[2 + n][0:m, :]).then_inc(ev, 1)
                act.wait_ge(less, 1)
                nc.scalar.activation(ex[:, :, :], lo[:, :, :], ACT.Exp).then_inc(exd, 1)

            @block.vector
            def _(dve):
                step = Chain(dve, step_s)
                nc.vector.memset(pos[:, :, :], 0.0)
                step(nc.vector.memset(lo[:, :, :], 0.0))
                dve.wait_ge(mm, 1)
                nc.vector.tensor_copy(lo[:, 0:2, :], bank[0][:, 0:2 * NE].rearrange("p (t e) -> p t e", e=NE))
                step(nc.vector.tensor_copy(lo[0:NS, 2, :], bank[0][0:NS, 2 * NE:3 * NE]))
                by_i, by_j = lo[:, :, :].unsqueeze(2).to_broadcast([P, 3, NE, NE]), lo[:, :, :].unsqueeze(3).to_broadcast([P, 3, NE, NE])
                nc.vector.tensor_tensor(above[:, :, :, :], by_i, by_j, ALU.is_gt)
                step(nc.vector.tensor_tensor(tie[:, :, :, :], by_i, by_j, ALU.is_equal))
                dve.wait_ge(made, 3)
                step(nc.vector.tensor_tensor(tie[:, :, :, :], tie[:, :, :, :],
                                             first[:, :, :].unsqueeze(1).to_broadcast([P, 3, NE, NE]), ALU.mult))
                step(nc.vector.tensor_tensor(above[:, :, :, :], above[:, :, :, :], tie[:, :, :, :], ALU.add))
                step(nc.vector.reduce_sum(rank[:, :, :], above[:, :, :, :], axis=AX))
                nc.vector.tensor_scalar(pick[:, :, :], rank[:, :, :], 1.5, None, ALU.is_lt).then_inc(picked, 1)
                step(nc.vector.reduce_max(top[:, :], lo[:, :, :], axis=AX))
                nc.vector.tensor_tensor(lo[:, :, :], lo[:, :, :], top[:, :].unsqueeze(2).to_broadcast([P, 3, NE]),
                                        ALU.subtract).then_inc(less, 1)
                dve.wait_ge(exd, 1)
                dve.wait_ge(picked, 1)
                step(nc.vector.tensor_tensor(ex[:, :, :], ex[:, :, :], pick[:, :, :], ALU.mult))
                step(nc.vector.reduce_sum(den[:, :], ex[:, :, :], axis=AX))
                step(nc.vector.reciprocal(top[:, :], den[:, :]))
                nc.vector.tensor_tensor(M.gate[:, :, :].rearrange("p e t -> p t e"), ex[:, :, :],
                                        top[:, :].unsqueeze(2).to_broadcast([P, 3, NE]), ALU.mult)
                nc.vector.tensor_copy(M.slots[:, :], num[:, :])
                dve.wait_ge(placed, 1)
                nc.vector.tensor_copy(pos[:, 0:2, :], bank[1][:, 0:2 * NE].rearrange("p (t e) -> p t e", e=NE))
                for tau in range(1, TAU):
                    nc.vector.tensor_scalar(more[:, NE * (tau - 1):NE * tau], bank[1][0:1, 3 * NE:4 * NE],
                                            128.0 * tau, None, ALU.is_gt)
                step(nc.vector.tensor_copy(pos[0:NS, 2, :], bank[1][0:NS, 2 * NE:3 * NE]))
                step(nc.vector.scalar_tensor_tensor(out=pos[:, :, :], in0=pos[:, :, :], scalar=1.0, in1=pick[:, :, :],
                                                    op0=ALU.add, op1=ALU.mult))
                for tau in range(TAU):
                    nc.vector.tensor_scalar(M.slot[:, NE * tau:NE * tau + NE, :].rearrange("p e t -> p t e"), pos[:, :, :],
                                            -1.0 - P * tau, None, ALU.add)
                nc.vector.tensor_copy(M.more[:, 0:2 * NE], more[:, :])
                step(nc.vector.reduce_max(some[:, :], more[:, :], axis=AX))
                nc.vector.tensor_copy(M.more[:, 2 * NE:], some[:, :])
                step(nc.vector.tensor_copy(acc[:, 0, :], more[:, :]))
                for i in range(4):
                    a, b, w = i % 2, 1 - i % 2, 1 << i
                    nc.vector.tensor_copy(acc[:, b, 0:w], acc[:, a, 0:w])
                    step(nc.vector.tensor_tensor(acc[:, b, w:], acc[:, a, w:], acc[:, a, 0:2 * NE - w], ALU.add))
                step(nc.vector.tensor_tensor(acc[:, 0, :], acc[:, 0, :], more[:, :], ALU.subtract))
                nc.vector.tensor_scalar(M.order[:, :], acc[:, 0, :], float(NE), None, ALU.add)


def stage_moe(nc, G, M, io):
    with Scope(nc, "moe") as s:
        RGU, RD, PAIR = 3, 2, GW // P
        wgu, wd = s.sb("w_gate_up", [P, RGU, DC, 2 * GW]), s.sb("w_down", [P, RD, PAIR, D])
        wgu_hi, wgu_lo = (s.sb(n, [P, 2, DC, 2 * GW], F32R) for n in ("w_gate_up_hi", "w_gate_up_lo"))
        wd_hi, wd_lo = (s.sb(n, [P, 2, PAIR, D], F32R) for n in ("w_down_hi", "w_down_lo"))
        xe_hi, xe_lo = s.sb("x_block_hi", [P, DC, P], F32R), s.sb("x_block_lo", [P, DC, P], F32R)
        y = s.sb("y_block", [P, D])
        H, silu_b = (y[:, 512 * i:512 * i + 512].rearrange("p (a n) -> p a n", n=GW) for i in range(2))
        HT_hi, HT_lo = s.sb("hidden_t_hi", [P, 2, GW], F32R), s.sb("hidden_t_lo", [P, 2, GW], F32R)
        sel, selg, selt = s.sb("sel", [P, 3, P]), s.sb("sel_gate", [P, 3, P]), s.sb("sel_gate_t", [P, NT])
        bank = [s.bank(f"b{i}") for i in range(8)]
        gu_in, d_in = [s.sem(f"gate_up_in{i}") for i in range(RGU)], [s.sem(f"down_in{i}") for i in range(RD)]
        selected, gathered, xe_high, xe_ready, sel_turned, selt_ready = (s.sem(n) for n in (
            "selected", "gathered", "x_high", "x_ready", "sel_turned", "sel_t_ready"))
        gu_high, gu_ready, d_high, d_ready = (s.sem(n) for n in ("gate_up_high", "gate_up_ready", "down_high", "down_ready"))
        gu, silu, hid, turned, ht_high, ht, used, y_ready, spread, added = (s.sem(n) for n in (
            "gate_up", "silu", "hidden", "hidden_turned", "hidden_t_high", "hidden_t_ready", "groups_used", "y_ready",
            "spread", "added"))
        freed = s.sem("slots_freed")

        def blocks(eng, body):
            with eng.Fori(0, NE) as e:
                body(e, e, e)
            some = eng.value_load(M.more[0:1, 2 * NE:2 * NE + 1], min_val=0, max_val=1)
            with eng.If(some > 0):
                with eng.Fori(1, TAU) as tau:
                    with eng.Fori(0, NE) as e:
                        at = tau * NE - NE + e
                        more = eng.value_load(M.more[0:1, bass.ds(at, 1)], min_val=0, max_val=1)
                        with eng.If(more > 0):
                            n = eng.value_load(M.order[0:1, bass.ds(at, 1)], min_val=NE, max_val=TAU * NE)
                            body(e, at + NE, n)

        AHEAD = 2

        def arrived(n, g, ring):
            return len(range(g % ring, NG, ring)) * n + g // ring + 1

        def former(g, ring):
            return NG + g - ring + 1 if g >= ring else max(range(g % ring, NG, ring)) + 1

        with nc.Block() as block:
            @block.sync
            def _(sp):
                def load_gate_up(e, n, g):
                    sp.wait_ge(gu_ready, NG * n + former(g, RGU))
                    sp.sem_inc(freed, 1)
                    for i, name in enumerate(("moe_w_gate", "moe_w_up")):
                        sp.dma_start(wgu[:, g % RGU, :, GW * i:GW * i + GW], io[name][0, bass.ds(e, 1), :, GW * g:GW * g + GW]
                                     .rearrange("o (k p) n -> p (o k) n", p=P)).then_inc(gu_in[g % RGU], 16)

                def load_down(e, n, g):
                    sp.wait_ge(d_ready, NG * n + former(g, RD))
                    sp.sem_inc(freed, 1)
                    sp.dma_start(wd[:, g % RD], io["moe_w_down"][0, bass.ds(e, 1), GW * g:GW * g + GW, :]
                                 .rearrange("o (k p) n -> p (o k) n", p=P)).then_inc(d_in[g % RD], 16)

                def body(e, blk, n):
                    for g in range(NG + AHEAD):
                        if g < NG:
                            load_gate_up(e, n, g)
                        if g >= AHEAD:
                            load_down(e, n, g - AHEAD)
                blocks(sp, body)

            @block.tensor
            def _(pe):
                def turn(n, g):
                    pe.wait_ge(hid, 1 + NG * n + g + 1)
                    if g >= 2:
                        pe.wait_ge(ht, 1 + NG * n + g - 1)
                    if g == 1:
                        pe.wait_ge(selt_ready, n + 1)
                    for q in range(PAIR):
                        last = nc.tensor.transpose(bank[2 + g % 2][:, P * q:P * q + P], H[:, g % 2, P * q:P * q + P], G.ident[:, :])
                    last.then_inc(turned, 1)

                def down(n, g):
                    pe.wait_ge(ht, 1 + NG * n + g + 1)
                    pe.wait_ge(d_ready, NG + NG * n + g + 1)
                    if g == 0:
                        pe.wait_ge(y_ready, 1 + 2 * n)
                    for q in range(PAIR):
                        for half in range(2):
                            c, f = slice(512 * half, 512 * half + 512), slice(P * q, P * q + P)
                            last = product(nc, bank[4 + half][:, :], HT_hi[:, g % 2, f], HT_lo[:, g % 2, f], wd_hi[:, g % 2, q, c],
                                           wd_lo[:, g % 2, q, c], g == 0 and q == 0, g == NG - 1 and q == PAIR - 1)
                    last.then_inc(used, 1)

                def body(e, blk, n):
                    pe.wait_ge(selected, 2 * n + 1)
                    pe.wait_ge(added, 1 + DC * n)
                    for half in range(2):
                        for c in range(4):
                            col = P * (4 * half + c)
                            for t, m in TILES:
                                last = nc.tensor.matmul(bank[6 + half][:, P * c:P * c + P], M.xt[0:m, t, col:col + P],
                                                        sel[0:m, t, :], start=(t == 0), stop=(t == 2))
                        last.then_inc(gathered, 1)
                    pe.wait_ge(selected, 2 * n + 2)
                    pe.wait_ge(ht, 1 + NG * n)
                    for t, m in TILES:
                        last = nc.tensor.transpose(bank[3][:, P * t:P * t + m], selg[0:m, t, :], G.ident[0:m, 0:m])
                    last.then_inc(sel_turned, 1)
                    pe.wait_ge(xe_ready, 2 * n + 2)
                    for g in range(NG):
                        pe.wait_ge(gu_ready, NG + NG * n + g + 1)
                        if g >= 2:
                            pe.wait_ge(hid, 1 + NG * n + g - 1)
                        for k in range(DC):
                            last = product(nc, bank[g % 2][:, :], xe_hi[:, k, :], xe_lo[:, k, :], wgu_hi[:, g % 2, k, :],
                                           wgu_lo[:, g % 2, k, :], k == 0, k == DC - 1)
                        last.then_inc(gu, 1)
                        if g >= 1:
                            turn(n, g - 1)
                        if g >= 2:
                            down(n, g - 2)
                    turn(n, NG - 1)
                    down(n, NG - 2)
                    down(n, NG - 1)
                    for c in range(DC):
                        if c % 4 == 0:
                            pe.wait_ge(y_ready, 1 + 2 * n + c // 4 + 1)
                        if c >= 2:
                            pe.wait_ge(added, 1 + DC * n + c - 1)
                        nc.tensor.matmul(bank[6 + c % 2][:, 0:NT], y[:, P * c:P * c + P], selt[:, :], start=True, stop=True).then_inc(spread, 1)

                pe.sem_inc(used, NG)
                pe.sem_inc(gu, NG)
                for sem in (gathered, sel_turned, turned, spread):
                    pe.sem_inc(sem, 1)
                blocks(pe, body)

            @block.scalar
            def _(act):
                def gate_up_high(n, g):
                    act.wait_ge(gu_in[g % RGU], 32 * arrived(n, g, RGU))
                    act.wait_ge(gu, NG * n + NG + max(g - 1, 0))
                    nc.scalar.copy(wgu_hi[:, g % 2], wgu[:, g % RGU]).then_inc(gu_high, 1)

                def down_high(n, g):
                    act.wait_ge(d_in[g % RD], 16 * arrived(n, g, RD))
                    act.wait_ge(used, NG * n + NG + max(g - 1, 0))
                    nc.scalar.copy(wd_hi[:, g % 2], wd[:, g % RD]).then_inc(d_high, 1)

                def hidden_t(n, g):
                    act.wait_ge(turned, 1 + NG * n + g + 1)
                    act.wait_ge(used, NG * n + NG + g - 1)
                    nc.scalar.copy(HT_hi[:, g % 2, :], bank[2 + g % 2][:, 0:GW]).then_inc(ht_high, 1)

                def body(e, blk, n):
                    gate_up_high(n, 0)
                    for half in range(2):
                        act.wait_ge(gathered, 1 + 2 * n + half + 1)
                        nc.scalar.copy(xe_hi[:, 4 * half:4 * half + 4, :].rearrange("p c s -> p (c s)"), bank[6 + half][:, :]).then_inc(xe_high, 1)
                    gate_up_high(n, 1)
                    for g in range(NG):
                        act.wait_ge(gu, NG * n + NG + g + 1)
                        act.wait_ge(hid, 1 + NG * n + max(g - 1, 0))
                        nc.scalar.activation(silu_b[:, g % 2, :], bank[g % 2][:, 0:GW], ACT.Silu).then_inc(silu, 1)
                        if g >= 1:
                            hidden_t(n, g - 1)
                        if g + 2 < NG:
                            gate_up_high(n, g + 2)
                        down_high(n, g)
                    hidden_t(n, NG - 1)
                    act.wait_ge(used, NG * n + 2 * NG)
                    act.wait_ge(spread, 1 + DC * n)
                    for half in range(2):
                        nc.scalar.copy(y[:, 512 * half:512 * half + 512], bank[4 + half][:, :]).then_inc(y_ready, 1)
                act.sem_inc(y_ready, 1)
                blocks(act, body)

            @block.vector
            def _(dve):
                def less(out, x, high):
                    return nc.vector.tensor_tensor(out, x, high, ALU.subtract)

                def gate_up_low(n, g):
                    dve.wait_ge(gu_high, NG * n + g + 1)
                    less(wgu_lo[:, g % 2], wgu[:, g % RGU], wgu_hi[:, g % 2]).then_inc(gu_ready, 1)

                def down_low(n, g):
                    dve.wait_ge(d_high, NG * n + g + 1)
                    less(wd_lo[:, g % 2], wd[:, g % RD], wd_hi[:, g % 2]).then_inc(d_ready, 1)

                def hidden_t_low(n, g):
                    dve.wait_ge(ht_high, NG * n + g + 1)
                    less(HT_lo[:, g % 2, :], bank[2 + g % 2][:, 0:GW], HT_hi[:, g % 2, :]).then_inc(ht, 1)

                def body(e, blk, n):
                    dve.wait_ge(gathered, 1 + 2 * n)
                    nc.vector.tensor_tensor(sel[:, :, :].unsqueeze(1), M.slots[:, :].unsqueeze(1).unsqueeze(1).to_broadcast([P, 1, 3, P]),
                                            M.slot[:, bass.ds(blk, 1), :].unsqueeze(3).to_broadcast([P, 1, 3, P]),
                                            ALU.is_equal).then_inc(selected, 1)
                    dve.wait_ge(selected, 2 * n + 1)
                    dve.wait_ge(sel_turned, 1 + n)
                    nc.vector.tensor_tensor(selg[:, :, :].unsqueeze(1), sel[:, :, :].unsqueeze(1),
                                            M.gate[:, bass.ds(e, 1), :].unsqueeze(3).to_broadcast([P, 1, 3, P]),
                                            ALU.mult).then_inc(selected, 1)
                    gate_up_low(n, 0)
                    for half in range(2):
                        dve.wait_ge(xe_high, 2 * n + half + 1)
                        cs = slice(4 * half, 4 * half + 4)
                        less(xe_lo[:, cs, :].rearrange("p c s -> p (c s)"), bank[6 + half][:, :],
                             xe_hi[:, cs, :].rearrange("p c s -> p (c s)")).then_inc(xe_ready, 1)
                    dve.wait_ge(sel_turned, 1 + n + 1)
                    dve.wait_ge(spread, 1 + DC * n)
                    nc.vector.tensor_copy(selt[:, :], bank[3][:, 0:NT]).then_inc(selt_ready, 1)
                    gate_up_low(n, 1)
                    for g in range(NG):
                        dve.wait_ge(silu, NG * n + g + 1)
                        dve.wait_ge(turned, 1 + NG * n + max(g - 1, 0))
                        nc.vector.tensor_tensor(H[:, g % 2, :], silu_b[:, g % 2, :], bank[g % 2][:, GW:2 * GW], ALU.mult).then_inc(hid, 1)
                        if g >= 1:
                            hidden_t_low(n, g - 1)
                        if g + 2 < NG:
                            gate_up_low(n, g + 2)
                        down_low(n, g)
                    hidden_t_low(n, NG - 1)
                    dve.wait_ge(added, 1 + DC * n)
                    for c in range(DC):
                        dve.wait_ge(spread, 1 + DC * n + c + 1)
                        nc.vector.tensor_tensor(G.h[:, c, :], G.h[:, c, :], bank[6 + c % 2][:, 0:NT], ALU.add).then_inc(added, 1)
                for sem in (hid, added, ht):
                    dve.sem_inc(sem, 1)
                for sem in (gu_ready, d_ready):
                    dve.sem_inc(sem, NG)
                blocks(dve, body)


def stage_store(nc, G, io):
    with Scope(nc, "store") as s:
        rows = s.sb("rows", [P, 3, D])
        bank = [s.bank(f"b{i}") for i in range(6)]
        turned, ev_a, ev_v, out = s.sem("turned"), s.sem("copied_act"), s.sem("copied_dve"), s.sem("y_out")
        with nc.Block() as block:
            @block.tensor
            def _(pe):
                for n in range(6):
                    t, m = n // 2, P if n < 4 else NS
                    for c in range(4):
                        last = nc.tensor.transpose(bank[n][0:m, P * c:P * c + P], G.h[:, 4 * (n % 2) + c, P * t:P * t + m],
                                                   G.ident[:, :])
                    last.then_inc(turned, 1)

            def copy(n, f):
                t, m = n // 2, P if n < 4 else NS
                return f(rows[0:m, t, 512 * (n % 2):512 * (n % 2) + 512], bank[n][0:m, :])

            @block.vector
            def _(dve):
                for n in range(0, 6, 2):
                    dve.wait_ge(turned, n + 1)
                    copy(n, nc.vector.tensor_copy).then_inc(ev_v, 1)

            @block.scalar
            def _(act):
                for n in range(1, 6, 2):
                    act.wait_ge(turned, n + 1)
                    copy(n, nc.scalar.copy).then_inc(ev_a, 1)

            @block.sync
            def _(sp):
                for t in range(3):
                    sp.wait_ge(ev_v, t + 1)
                    sp.wait_ge(ev_a, t + 1)
                    if t < 2:
                        sp.dma_start(io["y_prompt"][0, P * t:P * t + P, :], rows[:, t, :]).then_inc(out, 16)
                    else:
                        sp.dma_start(io["y_sample"].rearrange("b t d -> (b t) d"), rows[0:NS, 2, :]).then_inc(out, 16)
                sp.wait_ge(out, 48)


INS = ["x_prompt", "x_sample", "cache_cmp_kv", "cache_slc_kv", "state_win_kv", "state_wkv", "state_shift", "page_table",
       "norm_g", "rw_mix", "rw_vec", "rw_w_rkv", "rw_w_o", "rw_decay_w1", "rw_decay_w2", "rw_iclr_w1", "rw_iclr_w2",
       "rw_gate_w1", "rw_gate_w2", "ffn_w_gate", "ffn_w_up", "ffn_w_down", "moe_router", "moe_w_gate", "moe_w_up",
       "moe_w_down", "kv_norm_g", "w_kv", "k_norm_g", "cmp_pe", "cmp_w1", "cmp_w2", "w_qg", "q_norm_g", "w_o"]
OUTS = [("y_prompt", (1, NP, D)), ("y_sample", (NB, DS, D)),
        ("cmp_kv_prompt", (1, NP, 2, 4, 64)), ("cmp_kv_sample", (NB, DS, 2, 4, 64)),
        ("slc_kv_prompt", (1, NP, 2, 4, 64)), ("slc_kv_sample", (NB, DS, 2, 4, 64)),
        ("win_kv_prompt", (1, NP, 2, 4, 64)), ("win_kv_sample", (NB, 512, 2, 4, 64)),
        ("wkv_prompt", (1, 1, NH, 64, 64)), ("wkv_sample", (1, NB, NH, 64, 64)),
        ("shift_prompt", (1, 1, D)), ("shift_sample", (1, NB, D))]


class Bag:
    pass


def build(nc, io):
    with Scope(nc, "g") as s:
        G = Bag()
        G.h = s.sb("h", [P, DC, NT])
        G.ident, G.ones, G.blk = (s.sb(n, [P, P]) for n in ("ident", "ones", "blk"))
        G.eps, G.gneps = s.sb("eps", [P, 1]), s.sb("gneps", [P, 1])
        G.pv = s.sb("pv", [P, NCOL])
        with Scope(nc, "heads") as hd:
            G.head_of, G.to_head = hd.sb("head_of", [P, DC, NH], side="right"), hd.sb("to_head", [NH, DC, P], side="right")
            with Scope(nc, "masks") as s0:
                G.mask_su, G.mask_iu = (s0.sb(n, [P, P], side="right") for n in ("mask_su", "mask_iu"))
                G.level = s0.sb("level", [P, 8, P], side="right")
                stage_load(nc, G, io)

                with Scope(nc, "rw") as r:
                    R, W = Bag(), Bag()
                    R.g, W.bonus = r.sb("g", [P, DC, NT]), r.sb("bonus", [P, DC, NT])
                    with Scope(nc, "ri") as ri:
                        R.r, R.k, R.v, R.sg, R.a = (ri.sb(n, [P, DC, NT], side="right") for n in ("r", "k", "v", "sg", "a"))
                        stage_rwkv_in(nc, G, R, io, W.bonus)
                        W.ar, W.bt, W.kt = r.sb("ar", [P, DC, 2, NP]), r.sb("bt", [P, DC, NP]), r.sb("kt", [P, DC, NP])
                        W.vt, W.bht, W.kht = (r.sb(n, [P, 2, D]) for n in ("vt", "bht", "kht"))
                        W.wc, W.sv = r.sb("wc", [P, DC, NP // CH]), r.sb("sv", [P, 6, DS, HD])
                        stage_derive(nc, G, R, W)
                    stage_wkv(nc, G, R, W, io, r)
                    stage_rwkv_out(nc, G, R, W, io)
            stage_ffn(nc, G, io)

            with Scope(nc, "nsa") as n:
                K, Q = Bag(), Bag()
                K.vn, K.kt = n.sb("v_rows", [P, 3, 2, 2 * P]), n.sb("k_t", [P, 4, NT])
                K.idx = n.sb("cache_rows", [P, NB], I32)
                Q.o, Q.gs = n.sb("o", [P, DC, NT]), n.sb("gate_smp", [P, 3, DC, NS])
                Q.q2 = n.sb("q2", [P, 2 * NB, 64])
                Q.mask_slc, Q.mask_win, Q.mask_new = n.sb("mask_slc", [64, NB, 32]), n.sb("mask_win", [64, 512]), n.sb("mask_new", [64, NB, 32])
                with Scope(nc, "cp") as c:
                    K.kc, K.vc = c.sb("k_cmp", [P, NSEQ, 2, P]), c.sb("v_cmp", [P, NSEQ, 2 * P])
                    with Scope(nc, "cw") as w:
                        K.w1, K.w2, K.per = w.sb("w1", [P, 2, 2 * SUB, P]), w.sb("w2", [P, 2, P]), w.sb("pe_rows", [4 * SUB, P])
                        K.zeroed, K.cmp_in = w.sem("zeroed"), w.sem("compress_weights_in")
                        stage_index(nc, G, K, io)
                        stage_kv(nc, G, K, io)
                        stage_compress(nc, G, K, io)
                    Q.q, Q.gates, Q.covers = c.sb("q", [P, DC, NT]), c.sb("gates", [48, NT]), c.sb("covers", [P, NBLK])
                    Q.mask_a, Q.mask_b = c.sb("mask_a", [P, 512]), c.sb("mask_b", [P, 288])
                    Q.gp = c.sb("gate_prm", [P, 3, DC, NP])
                    stage_query(nc, G, K, Q, io)
                    stage_select(nc, G, K, Q, io)
                    K.Z, K.z_in = n.sb("rows_ab", [P, 2, RW], side="right"), [n.sem(f"rows_in{i}") for i in range(3)]
                    stage_prompt(nc, G, K, Q, io)
                stage_sample(nc, G, K, Q, io)
                stage_attn_out(nc, G, Q, io)

        with Scope(nc, "m") as m:
            M = Bag()
            M.xt, M.gate, M.slots = m.sb("x_rows", [P, 3, D]), m.sb("gate", [P, NE, 3]), m.sb("slot_row", [P, P])
            M.slot = m.sb("slot_in_block", [P, TAU * NE, 3])
            M.more, M.order = m.sb("runs", [1, 2 * NE + 1], I32), m.sb("blocks_before", [1, 2 * NE], I32)
            stage_route(nc, G, M, io)
            stage_moe(nc, G, M, io)
        stage_store(nc, G, io)


def kernel(**inputs):
    import numpy as _np
    import concourse.bacc as _bacc
    from concourse.bass_utils import run_bass_kernel_spmd as _run

    nc = _bacc.Bacc("TRN2", target_bir_lowering=False, num_devices=1)
    arrays, io = {}, {}
    for name in INS:
        a = _np.ascontiguousarray(inputs[name])
        arrays[f"in_{name}"] = a
        io[name] = nc.dram_tensor(f"in_{name}", a.shape, mybir.dt.from_np(a.dtype), kind="ExternalInput").ap()
    for name, shape in OUTS:
        io[name] = nc.dram_tensor(f"out_{name}", shape, F32, kind="ExternalOutput").ap()
    build(nc, io)
    r = _run(nc, [arrays], core_ids=[0])
    return tuple(r.results[0][f"out_{name}"] for name, _ in OUTS)
```
